# Optimizing a Trainium2 kernel written in Bass

```python
import math
import jax, jax.numpy as jnp
from jax import lax
import numpy as np

D_MODEL = 2048
BATCH = 1
SEQ = 256
DEPTH = 2

N_MIXERS = 3
EPS = 1e-6
Q_BLOCK = 128

MLSTM_HEADS = 8
MLSTM_DV = D_MODEL // MLSTM_HEADS
MLSTM_DQK = MLSTM_DV // 2
MLSTM_CHUNK = 128
MLSTM_CONV = 3
MLSTM_QK_CH = 2 * MLSTM_HEADS * MLSTM_DQK
MLSTM_COLS = MLSTM_QK_CH + 2 * MLSTM_HEADS * MLSTM_DV + 4 * MLSTM_HEADS

MLA_HEADS = D_MODEL // 128
MLA_NOPE = 128
MLA_ROPE = 64
MLA_DV = 128
MLA_KV_RANK = 512
ROPE_BASE = 10000.0
MLA_COLS = MLA_HEADS * (MLA_NOPE + MLA_ROPE) + MLA_KV_RANK + MLA_ROPE

DIL_GROUPS = ((128, 1), (512, 4), (2048, 16))
DIL_HEADS = D_MODEL // 256
DIL_DH = 128
DIL_COLS = len(DIL_GROUPS) * 3 * DIL_HEADS * DIL_DH

N_EXPERTS = 16
N_GROUPS = 4
EXPERTS_PER_GROUP = N_EXPERTS // N_GROUPS
TOP_K = 2
D_EXPERT = D_MODEL // 4

kernel_name = "hybrid_mlstm_mla_dilated_moe_encoder"

def rmsnorm(x, g):
    xf = x.astype(jnp.float32)
    y = xf * lax.rsqrt(jnp.mean(xf * xf, axis=-1, keepdims=True) + EPS)
    return (y * g.astype(jnp.float32)).astype(x.dtype)

def centred_depthwise_conv(x, w):
    c = x.shape[-1]
    return lax.conv_general_dilated(x, w[:, None, :].astype(x.dtype), window_strides=(1,), padding='SAME',
                                    dimension_numbers=('NWC', 'WIO', 'NWC'), feature_group_count=c)

def rope(x, pos):
    half = x.shape[-1] // 2
    inv = ROPE_BASE ** (-jnp.arange(half, dtype=jnp.float32) / half)
    ang = pos.astype(jnp.float32)[:, None] * inv[None, :]
    cos = jnp.cos(ang)[None, :, None, :]
    sin = jnp.sin(ang)[None, :, None, :]
    x1, x2 = x[..., :half], x[..., half:]
    return jnp.concatenate([x1 * cos - x2 * sin, x2 * cos + x1 * sin], axis=-1).astype(x.dtype)

def alibi_slopes(n):
    return jnp.exp2(-8.0 * jnp.arange(1, n + 1, dtype=jnp.float32) / n)

def mlstm_chunkwise(q, k, v, li, lf):
    bsz, nh, s, dk = q.shape
    dv = v.shape[-1]
    L = MLSTM_CHUNK
    nc = s // L
    f32 = jnp.float32
    qc = q.astype(f32).reshape(bsz, nh, nc, L, dk)
    kc = k.astype(f32).reshape(bsz, nh, nc, L, dk)
    vc = v.astype(f32).reshape(bsz, nh, nc, L, dv)
    lic = li.reshape(bsz, nh, nc, L)
    b = jnp.cumsum(lf.reshape(bsz, nh, nc, L), axis=-1)
    g = b[..., -1]
    lower = jnp.tril(jnp.ones((L, L), dtype=bool))
    dlog = jnp.where(lower, b[..., :, None] - b[..., None, :] + lic[..., None, :], -jnp.inf)
    m_intra = jnp.max(dlog, axis=-1)
    w = g[..., None] - b + lic
    m_loc = jnp.max(w, axis=-1)
    ew = jnp.exp(w - m_loc[..., None])
    c_loc = jnp.einsum('bhcl,bhcld,bhcle->bhcde', ew, kc, vc)
    n_loc = jnp.einsum('bhcl,bhcld->bhcd', ew, kc)

    def step(carry, xs):
        c_st, n_st, m_st = carry
        g_c, ml_c, cl_c, nl_c = xs
        m_new = jnp.maximum(g_c + m_st, ml_c)
        a = jnp.exp(g_c + m_st - m_new)
        e = jnp.exp(ml_c - m_new)
        c_new = a[..., None, None] * c_st + e[..., None, None] * cl_c
        n_new = a[..., None] * n_st + e[..., None] * nl_c
        return (c_new, n_new, m_new), (c_st, n_st, m_st)

    init = (jnp.zeros((bsz, nh, dk, dv), f32), jnp.zeros((bsz, nh, dk), f32), jnp.zeros((bsz, nh), f32))
    xs = (jnp.moveaxis(g, 2, 0), jnp.moveaxis(m_loc, 2, 0), jnp.moveaxis(c_loc, 2, 0), jnp.moveaxis(n_loc, 2, 0))
    _, (c_prev, n_prev, m_prev) = lax.scan(step, init, xs)
    c_prev = jnp.moveaxis(c_prev, 0, 2)
    n_prev = jnp.moveaxis(n_prev, 0, 2)
    m_prev = jnp.moveaxis(m_prev, 0, 2)

    a_inter = b + m_prev[..., None]
    m = jnp.maximum(a_inter, m_intra)
    e_inter = jnp.exp(a_inter - m)
    dmat = jnp.exp(dlog - m[..., None]) * jnp.einsum('bhcld,bhcsd->bhcls', qc, kc)
    num = e_inter[..., None] * jnp.einsum('bhcld,bhcde->bhcle', qc, c_prev) + jnp.einsum('bhcls,bhcse->bhcle', dmat, vc)
    den = e_inter * jnp.einsum('bhcld,bhcd->bhcl', qc, n_prev) + jnp.sum(dmat, axis=-1)
    h = num / jnp.maximum(jnp.abs(den), jnp.exp(-m))[..., None]
    return h.reshape(bsz, nh, s, dv)

def mlstm_mixer(xn, w_in, conv_w, gate_b, out_norm, w_out):
    bsz, s, _ = xn.shape
    H = MLSTM_HEADS
    p = xn @ w_in
    qk = jax.nn.silu(centred_depthwise_conv(p[..., :MLSTM_QK_CH], conv_w))
    off = MLSTM_QK_CH
    v = p[..., off:off + H * MLSTM_DV]
    o = p[..., off + H * MLSTM_DV:off + 2 * H * MLSTM_DV]
    gates = p[..., off + 2 * H * MLSTM_DV:].astype(jnp.float32) + gate_b.astype(jnp.float32)
    gates = gates.reshape(bsz, s, 4, H).transpose(2, 0, 3, 1)
    q = qk[..., :H * MLSTM_DQK].reshape(bsz, s, H, MLSTM_DQK).transpose(0, 2, 1, 3) * (MLSTM_DQK ** -0.5)
    k = qk[..., H * MLSTM_DQK:].reshape(bsz, s, H, MLSTM_DQK).transpose(0, 2, 1, 3)
    v = v.reshape(bsz, s, H, MLSTM_DV).transpose(0, 2, 1, 3)
    h_f = mlstm_chunkwise(q, k, v, gates[0], jax.nn.log_sigmoid(gates[1]))
    flip = lambda t: jnp.flip(t, axis=2)
    h_b = flip(mlstm_chunkwise(flip(q), flip(k), flip(v), jnp.flip(gates[2], -1),
                               jnp.flip(jax.nn.log_sigmoid(gates[3]), -1)))
    h = (h_f + h_b).astype(xn.dtype).transpose(0, 2, 1, 3)
    h = rmsnorm(h, out_norm.reshape(H, MLSTM_DV)).reshape(bsz, s, H * MLSTM_DV)
    return (jax.nn.sigmoid(o) * h) @ w_out

def dense_block_attention(q, k, v, scale):
    bsz, s, nh, dq = q.shape
    dv = v.shape[-1]
    nb = s // Q_BLOCK
    qb = q.reshape(bsz, nb, Q_BLOCK, nh, dq).swapaxes(0, 1)

    def one(qblk):
        sc = jnp.einsum('bqhd,bkhd->bhqk', qblk, k).astype(jnp.float32) * scale
        pr = jax.nn.softmax(sc, axis=-1).astype(v.dtype)
        return jnp.einsum('bhqk,bkhd->bqhd', pr, v)

    o = lax.map(one, qb)
    return o.swapaxes(0, 1).reshape(bsz, s, nh, dv)

def mla_mixer(xn, w_in, kv_norm, w_ukv, q_norm, k_norm, w_out):
    bsz, s, _ = xn.shape
    H = MLA_HEADS
    dqk = MLA_NOPE + MLA_ROPE
    p = xn @ w_in
    q = p[..., :H * dqk].reshape(bsz, s, H, dqk)
    ckv = p[..., H * dqk:H * dqk + MLA_KV_RANK]
    k_rope = p[..., H * dqk + MLA_KV_RANK:]
    kv = (rmsnorm(ckv, kv_norm) @ w_ukv).reshape(bsz, s, H, MLA_NOPE + MLA_DV)
    k_nope, v = kv[..., :MLA_NOPE], kv[..., MLA_NOPE:]
    k = jnp.concatenate([k_nope, jnp.broadcast_to(k_rope[:, :, None, :], (bsz, s, H, MLA_ROPE))], axis=-1)
    q = rmsnorm(q, q_norm)
    k = rmsnorm(k, k_norm)
    pos = jnp.arange(s)
    q = jnp.concatenate([q[..., :MLA_NOPE], rope(q[..., MLA_NOPE:], pos)], axis=-1)
    k = jnp.concatenate([k[..., :MLA_NOPE], rope(k[..., MLA_NOPE:], pos)], axis=-1)
    o = dense_block_attention(q, k, v, dqk ** -0.5)
    return o.reshape(bsz, s, H * MLA_DV) @ w_out

def dilated_mixer(xn, w_in, q_norm, k_norm, w_out):
    bsz, s, _ = xn.shape
    G, H, dh = len(DIL_GROUPS), DIL_HEADS, DIL_DH
    p = (xn @ w_in).reshape(bsz, s, G, 3, H, dh)
    q = rmsnorm(p[:, :, :, 0], q_norm[:, None, :])
    k = rmsnorm(p[:, :, :, 1], k_norm[:, None, :])
    v = p[:, :, :, 2]
    slopes = alibi_slopes(G * H).reshape(G, H)
    scale = dh ** -0.5
    nb = s // Q_BLOCK
    qb = q.reshape(bsz, nb, Q_BLOCK, G, H, dh).swapaxes(0, 1)
    starts = jnp.arange(nb) * Q_BLOCK

    def one(args):
        qblk, t0 = args
        t = t0 + jnp.arange(Q_BLOCK)
        outs, lses = [], []
        for gi, (win, dil) in enumerate(DIL_GROUPS):
            side = win // (2 * dil)
            offs = dil * jnp.arange(-side, side + 1)
            pos = t[:, None] + offs[None, :]
            valid = (pos >= 0) & (pos < s)
            idx = jnp.clip(pos, 0, s - 1)
            kg = jnp.take(k[:, :, gi], idx, axis=1)
            vg = jnp.take(v[:, :, gi], idx, axis=1)
            sc = jnp.einsum('bqhd,bqjhd->bhqj', qblk[:, :, gi], kg).astype(jnp.float32) * scale
            sc = sc - slopes[gi][:, None, None] * jnp.abs(offs).astype(jnp.float32)[None, None, :]
            sc = jnp.where(valid[None, None], sc, -jnp.inf)
            mx = jnp.max(sc, axis=-1, keepdims=True)
            e = jnp.exp(sc - mx)
            den = jnp.sum(e, axis=-1)
            o = jnp.einsum('bhqj,bqjhd->bqhd', (e / den[..., None]).astype(v.dtype), vg)
            outs.append(o)
            lses.append(mx[..., 0] + jnp.log(den))
        wts = jax.nn.softmax(jnp.stack(lses, axis=0), axis=0)
        comb = outs[0] * wts[0].transpose(0, 2, 1)[..., None].astype(v.dtype)
        for gi in range(1, G):
            comb = comb + outs[gi] * wts[gi].transpose(0, 2, 1)[..., None].astype(v.dtype)
        return comb

    o = lax.map(one, (qb, starts))
    o = o.swapaxes(0, 1).reshape(bsz, s, H * dh)
    return o @ w_out

def moe_ffn(xn, router_w, router_b, w_gate, w_up, w_down):
    bsz, s, d = xn.shape
    xt = xn.reshape(bsz * s, d)
    scores = jax.nn.sigmoid((xt @ router_w).astype(jnp.float32))
    sel = scores + router_b.astype(jnp.float32)
    grp_score = jnp.sum(lax.top_k(sel.reshape(-1, N_GROUPS, EXPERTS_PER_GROUP), 2)[0], axis=-1)
    gmask = jax.nn.one_hot(jnp.argmax(grp_score, axis=-1), N_GROUPS, dtype=jnp.bool_)
    masked = jnp.where(jnp.repeat(gmask, EXPERTS_PER_GROUP, axis=-1), sel, -jnp.inf)
    _, eidx = lax.top_k(masked, TOP_K)
    w = jnp.take_along_axis(scores, eidx, axis=-1)
    w = w / jnp.sum(w, axis=-1, keepdims=True)
    gates = jnp.sum(jax.nn.one_hot(eidx, N_EXPERTS, dtype=jnp.float32) * w[..., None], axis=1)
    hg = jnp.einsum('td,edf->tef', xt, w_gate)
    hu = jnp.einsum('td,edf->tef', xt, w_up)
    a = jax.nn.silu(hg) * hu * gates[..., None].astype(xt.dtype)
    y = jnp.einsum('tef,efd->td', a, w_down)
    return y.reshape(bsz, s, d)

def setup_inputs(seed: int = 0) -> dict:
    key = jax.random.key(seed)
    ks = iter(jax.random.split(key, 32))
    nrm = lambda shape, std: jax.random.normal(next(ks), shape, jnp.float32) * std
    n_a = len(range(0, DEPTH, N_MIXERS))
    n_b = len(range(1, DEPTH, N_MIXERS))
    n_c = len(range(2, DEPTH, N_MIXERS))
    res = (2 * DEPTH) ** -0.5
    ib = nrm((n_a, 2, MLSTM_HEADS), 0.1)
    fb = 3.0 + nrm((n_a, 2, MLSTM_HEADS), 0.5)
    gate_b = jnp.stack([ib[:, 0], fb[:, 0], ib[:, 1], fb[:, 1]], axis=1).reshape(n_a, 4 * MLSTM_HEADS)
    dil_w_out_in = DIL_HEADS * DIL_DH
    return {
        "x": nrm((BATCH, SEQ, D_MODEL), 1.0),
        "norm_mix": 1.0 + nrm((DEPTH, D_MODEL), 0.02),
        "norm_ffn": 1.0 + nrm((DEPTH, D_MODEL), 0.02),
        "a_w_in": nrm((n_a, D_MODEL, MLSTM_COLS), D_MODEL ** -0.5),
        "a_conv_w": nrm((n_a, MLSTM_CONV, MLSTM_QK_CH), MLSTM_CONV ** -0.5),
        "a_gate_b": gate_b,
        "a_out_norm": 1.0 + nrm((n_a, MLSTM_HEADS * MLSTM_DV), 0.02),
        "a_w_out": nrm((n_a, MLSTM_HEADS * MLSTM_DV, D_MODEL), (MLSTM_HEADS * MLSTM_DV) ** -0.5 * res),
        "b_w_in": nrm((n_b, D_MODEL, MLA_COLS), D_MODEL ** -0.5),
        "b_kv_norm": 1.0 + nrm((n_b, MLA_KV_RANK), 0.02),
        "b_w_ukv": nrm((n_b, MLA_KV_RANK, MLA_HEADS * (MLA_NOPE + MLA_DV)), MLA_KV_RANK ** -0.5),
        "b_q_norm": 1.0 + nrm((n_b, MLA_NOPE + MLA_ROPE), 0.02),
        "b_k_norm": 1.0 + nrm((n_b, MLA_NOPE + MLA_ROPE), 0.02),
        "b_w_out": nrm((n_b, MLA_HEADS * MLA_DV, D_MODEL), (MLA_HEADS * MLA_DV) ** -0.5 * res),
        "c_w_in": nrm((n_c, D_MODEL, DIL_COLS), D_MODEL ** -0.5),
        "c_q_norm": 1.0 + nrm((n_c, len(DIL_GROUPS), DIL_DH), 0.02),
        "c_k_norm": 1.0 + nrm((n_c, len(DIL_GROUPS), DIL_DH), 0.02),
        "c_w_out": nrm((n_c, dil_w_out_in, D_MODEL), dil_w_out_in ** -0.5 * res),
        "router_w": nrm((D_MODEL, N_EXPERTS), D_MODEL ** -0.5),
        "router_b": nrm((N_EXPERTS,), 0.01),
        "moe_w_gate": nrm((DEPTH, N_EXPERTS, D_MODEL, D_EXPERT), D_MODEL ** -0.5),
        "moe_w_up": nrm((DEPTH, N_EXPERTS, D_MODEL, D_EXPERT), D_MODEL ** -0.5),
        "moe_w_down": nrm((DEPTH, N_EXPERTS, D_EXPERT, D_MODEL), D_EXPERT ** -0.5 * res),
    }

def reference(x, norm_mix, norm_ffn, a_w_in, a_conv_w, a_gate_b, a_out_norm, a_w_out,
              b_w_in, b_kv_norm, b_w_ukv, b_q_norm, b_k_norm, b_w_out,
              c_w_in, c_q_norm, c_k_norm, c_w_out,
              router_w, router_b, moe_w_gate, moe_w_up, moe_w_down):
    for i in range(DEPTH):
        kind = i % N_MIXERS
        j = i // N_MIXERS
        xn = rmsnorm(x, norm_mix[i])
        if kind == 0:
            y = mlstm_mixer(xn, a_w_in[j], a_conv_w[j], a_gate_b[j], a_out_norm[j], a_w_out[j])
        elif kind == 1:
            y = mla_mixer(xn, b_w_in[j], b_kv_norm[j], b_w_ukv[j], b_q_norm[j], b_k_norm[j], b_w_out[j])
        else:
            y = dilated_mixer(xn, c_w_in[j], c_q_norm[j], c_k_norm[j], c_w_out[j])
        x = x + y
        x = x + moe_ffn(rmsnorm(x, norm_ffn[i]), router_w, router_b, moe_w_gate[i], moe_w_up[i], moe_w_down[i])
    return x


_drawn_inputs = setup_inputs


def setup_inputs(seed=0):
    import zlib

    import numpy as np

    out = dict(_drawn_inputs(seed))
    spreads = {}
    factors = {'b_kv_norm': 7.877, 'b_q_norm': 4.779, 'b_k_norm': 3.025}
    for name, (base, spread) in spreads.items():
        noise = np.random.default_rng([zlib.crc32(name.encode()), seed]).standard_normal(out[name].shape)
        drawn = base * np.exp(spread * noise) if base else spread * noise
        out[name] = __import__('jax').numpy.asarray(drawn.astype(out[name].dtype))
    for name, factor in factors.items():
        out[name] = (out[name] * factor).astype(out[name].dtype)
    return out
```

```python
import concourse.bass as bass
from concourse import mybir
from contextlib import ExitStack

P = 128
D = 2048
SEQ = 256
NT = SEQ // P
DC = D // P
EPS = 1e-6
UNIT_K = 4
UNIT_C = 512
RING = 8
UNITS_PER_BLOCK = D // (UNIT_K * P)

HEADS_A = 8
DV_A = D // HEADS_A
DQK_A = DV_A // 2
QK_CH = 2 * HEADS_A * DQK_A
VW = DV_A + 2
N_GATES = 4 * HEADS_A

HEADS_B = 16
NOPE = 128
ROPE = 64
HALF = ROPE // 2
DQ_B = NOPE + ROPE
DV_B = 128
RANK = 512
RC = RANK // P
Q_COLS = HEADS_B * DQ_B

N_EXP = 16
N_GRP = 4
PER_GRP = N_EXP // N_GRP
F = 512
FC = F // P
PAIRS = N_EXP // 2
SLOTS = 64
EXTRA = SEQ // SLOTS - 1
PAIR_UNITS = 24

C_ID = 0
C_TRI = 128
C_ONE = 256
C_IOTA = 384
C_MASK = 640
C_LT = 896
C_COS = 912
C_SIN = C_COS + 2 * ROPE
C_ALL = C_SIN + 2 * ROPE
MASKED = 1e30

V_MIX = 0
V_FFN = 32
V_CONV = 64
V_KV = 112
V_ROWS = 116
V_OUT = 116
V_ALL = 132

U_QK = 0
U_V = U_QK + 16
U_O = U_V + 16
U_AOUT = U_O + 16
U_MOE0 = U_AOUT + 16
U_CKV = U_MOE0 + PAIRS * PAIR_UNITS
U_Q = U_CKV + 4
U_UKV = U_Q + 24
U_BOUT = U_UKV + 8
U_MOE1 = U_BOUT + 16
ROW = 40


NORMS = ("n0", "n1", "n2", "n3")
TURNS = ("n0", "h", "n1", "n2", "n3")


class Chain:

    def __init__(self, eng, sem, base=0):
        self.eng, self.sem, self.base, self.n = eng, sem, base, 0

    def __call__(self, ins):
        self.n += 1
        ins.then_inc(self.sem, 1)
        self.eng.wait_ge(self.sem, self.base + self.n)


def trunk(nc, w, out):
    f32 = mybir.dt.float32
    i32 = mybir.dt.int32
    ALU = mybir.AluOpType
    ACT = mybir.ActivationFunctionType
    AX = mybir.AxisListType
    ds = bass.ds

    ctx = ExitStack()
    with ctx:
        def sb(name, shape, dt=f32):
            return ctx.enter_context(nc.sbuf_tensor(name, shape, dt))

        sems = {}

        def sem(name):
            if name not in sems:
                sems[name] = ctx.enter_context(nc.semaphore(name))
            return sems[name]

        X = sb("X", [P, NT, D])
        XN = sb("XN", [P, NT, D])
        XT = sb("XT", [P, DC, SEQ])
        ring = [sb(f"ring{s}", [P, UNIT_K, UNIT_C]) for s in range(RING)]
        CON = sb("CON", [P, C_ALL])
        VEC = sb("VEC", [P, V_ALL])
        RW = sb("RW", [P, DC, N_EXP])
        RB = sb("RB", [P, N_EXP])
        SSQ = sb("SSQ", [P, 8])
        FLAG = sb("FLAG", [P, 2], i32)
        PS = ctx.enter_context(nc.psum_tensor("PS", [P, 8, 512], f32))
        IDENT = CON[:, C_ID:C_ID + P]
        TRI = CON[:, C_TRI:C_TRI + P]
        ONES = CON[:, C_ONE:C_ONE + P]

        AREA_W = 21600
        AREA = sb("AREA", [P, AREA_W])

        def carve(sizes):
            at, views = 0, {}
            for name, shape in sizes:
                n = 1
                for s in shape:
                    n *= s
                v = AREA[:, at:at + n]
                if len(shape) == 2:
                    v = v.rearrange("p (a b) -> p a b", a=shape[0])
                if len(shape) == 3:
                    v = v.rearrange("p (a b c) -> p a b c", a=shape[0], b=shape[1])
                views[name] = v
                at += n
            assert at <= AREA_W, at
            return views

        a_ = carve([
            ("JUNK", (D,)), ("QKT", (DC, SEQ)), ("VA", (NT, HEADS_A, VW)), ("OG", (NT, D)),
            ("WG", (DC, N_GATES)), ("PAD", (2, SEQ + 2)), ("CT", (2, SEQ)), ("SGC", (2, SEQ)),
            ("GP", (4, ROW)), ("LI", (SEQ,)), ("LF", (SEQ,)), ("T1", (SEQ,)), ("T2", (SEQ,)),
            ("B", (SEQ,)), ("R", (SEQ,)), ("RQ", (4, SEQ)), ("COLT", (8, ROW)), ("MP", (4,)),
            ("GB", (N_GATES,)),
            ("Z", (2, SEQ)), ("NS", (4, VW)), ("DEN", (8,)), ("DT", (2, SEQ))])
        a_.update(carve([("HQ", (2, SEQ)), ("RSEL", (2, SEQ)), ("KW", (2, P)), ("CS", (2, VW))]))
        b_ = carve([
            ("JUNK", (D,)), ("CKV", (NT, RANK)), ("WKR", (DC, ROPE)), ("Q", (NT, Q_COLS)), ("CKT", (RC, SEQ)),
            ("KV", (NT, HEADS_B * 2 * P)), ("QG", (DQ_B,)), ("KG", (DQ_B,)),
            ("KR", (NT, ROPE)), ("KRT", (NT, ROPE)), ("KRR", (NT, ROPE)), ("SS", (4, HEADS_B)),
            ("RN", (4, HEADS_B))])
        HB = [XN[:, :, :].rearrange("p t d -> p (t d)")[:, 0:3328], AREA[:, 0:3328]]
        m_ = carve([
            ("JUNK", (D,)), ("SEL", (2, P)), ("SELG", (2, P)), ("XG", (DC, P)), ("SIG", (F,)), ("A", (F,)),
            ("AT", (FC, P)), ("YS", (4, UNIT_C)), ("SCT", (SEQ,)),
            ("SC", (NT, N_EXP)), ("SR", (NT, N_EXP)), ("MK", (NT, N_EXP)), ("GATE", (NT, N_EXP)),
            ("KEY", (NT, N_EXP)), ("G1", (4 * N_EXP,)), ("G2", (4 * N_EXP,)), ("G3", (N_EXP,)),
            ("G4", (N_EXP,)), ("G5", (N_EXP,)), ("G6", (N_EXP,)),
            ("OV", (4 * UNIT_K, UNIT_C))])
        ov_ring = [m_["OV"][:, 4 * s:4 * s + 4, :] for s in range(4)]

        def hb(p, at, shape):
            n = 1
            for s in shape:
                n *= s
            v = HB[p][:, at:at + n]
            return v.rearrange("p (a b) -> p a b", a=shape[0]) if len(shape) == 2 else v

        QN = [hb(p, 0, (2, DQ_B)) for p in range(2)]
        KN = [hb(p, 384, (2, DQ_B)) for p in range(2)]
        ROT = [hb(p, 768, (2, ROPE)) for p in range(2)]
        ROS = [hb(p, 896, (2, ROPE)) for p in range(2)]
        VS = [hb(p, 1024, (2, DV_B)) for p in range(2)]
        QKN = [hb(p, 1280, (512,)) for p in range(2)]
        QKR = [hb(p, 1792, (512,)) for p in range(2)]
        PR = [hb(p, 2304, (2, SEQ)) for p in range(2)]
        PT = [hb(p, 2816, (2, SEQ)) for p in range(2)]
        SM = sb("SM", [P, 2, 8])
        SMA = sb("SMA", [P, 2, NT * HEADS_A])
        MPB = sb("MPB", [P, NT])
        ROWS = sb("ROWS", [P, P])
        ROWS2 = sb("ROWS2", [16, P])

        def vec(at, n=1):
            return VEC[:, ds(at, n)]

        def vec4(at):
            return VEC[:, at:at + 4].unsqueeze(2).broadcast_to([P, 4, P])

        def ps4(bank):
            return PS[:, bank, :].rearrange("p (a b) -> p a b", a=4)

        def unit_arrived(eng, u, i=0, per=8):
            eng.wait_ge(sem(f"unit_loaded_{u % RING}"), 16 * (u // RING + 1) + 16 * (per // RING) * i)

        block = ctx.enter_context(nc.Block())

        @block.sync
        def _(sp):
            used = sem("unit_used")

            def unit(u, src, i=0, per=8):
                if u >= RING:
                    sp.wait_ge(used, u - RING + 1 + per * i)
                sp.dma_start(ring[u % RING][:, :, :], src).then_inc(sem(f"unit_loaded_{u % RING}"), 16)

            def matrix(base, view, blocks, first_col):
                def body(i):
                    for n in range(8):
                        c = first_col + UNIT_C * (2 * i + n // 4)
                        unit(base + n, view[n % 4][:, :, ds(c, UNIT_C)], i)
                if base == 0:
                    body(0)
                    base, first_col, blocks = base + 8, first_col + 2 * UNIT_C, blocks - 2
                if blocks == 2:
                    body(0)
                else:
                    with sp.Fori(0, blocks // 2) as i:
                        body(i)

            def k_view(m):
                return m.rearrange("(q k p) c -> q p k c", p=P, k=UNIT_K)

            def experts(layer, base):
                wg, wu = (w[n][layer].rearrange("e (q k p) f -> e q p k f", p=P, k=UNIT_K)
                          for n in ("moe_w_gate", "moe_w_up"))
                wd = w["moe_w_down"][layer].rearrange("e (k p) c -> e p k c", p=P)
                with sp.Fori(0, PAIRS) as i:
                    n = 0
                    for q in range(4):
                        for m in (wg, wu):
                            for e in range(2):
                                unit(base + n, m[2 * i + e, q], i, PAIR_UNITS)
                                n += 1
                    for d in range(4):
                        for e in range(2):
                            unit(base + n, wd[2 * i + e][:, :, d * UNIT_C:(d + 1) * UNIT_C], i, PAIR_UNITS)
                            n += 1

            a_in = k_view(w["a_w_in"][0])
            matrix(U_QK, a_in, 4, 0)
            matrix(U_V, a_in, 4, QK_CH)
            matrix(U_O, a_in, 4, QK_CH + D)
            matrix(U_AOUT, k_view(w["a_w_out"][0]), 4, 0)
            experts(0, U_MOE0)
            b_in = k_view(w["b_w_in"][0])
            for n in range(4):
                unit(U_CKV + n, b_in[n][:, :, Q_COLS:Q_COLS + RANK])
            matrix(U_Q, b_in, 6, 0)
            ukv = w["b_w_ukv"][0].rearrange("(k p) c -> p k c", p=P)
            for n in range(8):
                unit(U_UKV + n, ukv[:, :, n * UNIT_C:(n + 1) * UNIT_C])
            matrix(U_BOUT, k_view(w["b_w_out"][0]), 4, 0)
            experts(1, U_MOE1)
            sp.wait_ge(sem("x_ready"), 16 + 4)
            sp.dma_start(out.rearrange("b (t p) d -> p (b t) d", p=P), X[:, :, :]).then_inc(sem("stored"), 16)
            sp.wait_ge(sem("stored"), 16)

        @block.gpsimd
        def _(pool):
            for l in range(2):
                pool.wait_ge(sem("routed"), l + 1)
                flag = pool.value_load(FLAG[0:1, l:l + 1], min_val=0, max_val=1)
                wg, wu = (w[n][l].rearrange("e (q k p) f -> e q p k f", p=P, k=UNIT_K)
                          for n in ("moe_w_gate", "moe_w_up"))
                wd = w["moe_w_down"][l].rearrange("e (k p) c -> e p k c", p=P)
                with pool.If(flag > 0):
                    with pool.Fori(0, EXTRA) as q:
                        with pool.Fori(0, PAIRS) as i:
                            j = q * PAIRS + i
                            srcs = [m[2 * i + e, k] for k in range(4) for m in (wg, wu) for e in range(2)]
                            srcs += [wd[2 * i + e][:, :, d * UNIT_C:(d + 1) * UNIT_C] for d in range(4) for e in range(2)]
                            for n, src in enumerate(srcs):
                                pool.wait_ge(sem(f"over_free_{l}"), j * PAIR_UNITS + n + 1)
                                pool.sem_inc(sem("over_turns"), 1)
                                pool.dma_start(ov_ring[n % 4], src).then_inc(sem(f"over_loaded_{l}_{n % 4}"), 16)

        @block.tensor
        def _(pe):
            used = sem("unit_used")

            def transposes(tag):
                for n in range(8):
                    t, g = divmod(n, 4)
                    if g == 0:
                        pe.wait_ge(sem("xn_ready"), NT * TURNS.index(tag) + t + 1)
                    for k in range(4):
                        c = 4 * g + k
                        last = pe.transpose(PS[:, n, k * P:(k + 1) * P], XN[:, t, c * P:(c + 1) * P], IDENT)
                    last.then_inc(sem("turned"), 1)

            def xt_ready(tag):
                pe.wait_ge(sem("xt_ready"), 8 * (TURNS.index(tag) + 1))

            def token_block(base, b, i, free, credit_at):
                pe.wait_ge(sem(free), credit_at)
                for n in range(4):
                    u = base + n
                    unit_arrived(pe, u, i)
                    for kk in range(UNIT_K):
                        for t in range(NT):
                            last = pe.matmul(PS[:, 2 * b + t, :], XT[:, UNIT_K * n + kk, t * P:(t + 1) * P],
                                             ring[u % RING][:, kk, :], start=(n == 0 and kk == 0),
                                             stop=(n == 3 and kk == UNIT_K - 1))
                    last.then_inc(used, 1)

            def token_product(base, turns, free):
                with pe.Fori(0, turns) as i:
                    for b in range(2):
                        token_block(base + 4 * b, b, i, free, 4 * i + 2 * b + 2)

            pe.wait_ge(sem("vectors_loaded"), 16 * 6)
            pe.wait_ge(sem("consts_loaded"), 16)
            pe.transpose(PS[:, 7, 0:V_ROWS], ROWS[0:V_ROWS, :], IDENT[0:V_ROWS, 0:V_ROWS])
            pe.transpose(PS[:, 7, 128:144], ROWS2[:, :], IDENT[0:16, 0:16]).then_inc(sem("vectors_turned"), 1)
            pe.wait_ge(sem("vec_ready"), 2)
            transposes("n0")
            xt_ready("n0")
            pe.wait_ge(sem("wg_loaded"), 16)
            for t in range(NT):
                for k in range(DC):
                    last = pe.matmul(PS[:, 7, t * N_GATES:(t + 1) * N_GATES], XT[:, k, t * P:(t + 1) * P],
                                     a_["WG"][:, k, :], start=(k == 0), stop=(k == DC - 1))
            last.then_inc(sem("gates_done"), 1)
            pe.wait_ge(sem("gates_read"), 2)
            with pe.Fori(0, 2) as i:
                for b in range(2):
                    for n in range(4):
                        u = U_QK + 4 * b + n
                        unit_arrived(pe, u, i)
                        for ch in range(4):
                            if n == 0:
                                pe.wait_ge(sem("qk_free"), 8 * i + 4 * b + ch + 1)
                            for kk in range(UNIT_K):
                                last = pe.matmul(PS[:, 4 * b + ch, 0:SEQ], ring[u % RING][:, kk, ch * P:(ch + 1) * P],
                                                 XT[:, UNIT_K * n + kk, :], start=(n == 0 and kk == 0),
                                                 stop=(n == 3 and kk == UNIT_K - 1))
                        last.then_inc(used, 1)
            pe.wait_ge(sem("qk_free"), 8 + 16)
            for n in range(4):
                ty, t = divmod(n, 2)
                last = pe.transpose(PS[0:ROW, 6, n * P:(n + 1) * P], a_["GP"][:, 2 * ty + t, :], IDENT)
            last.then_inc(sem("gate_rows"), 1)
            token_product(U_V, 2, "v_free")
            pe.wait_ge(sem("rows_ready"), 1)
            pe.wait_ge(sem("rows_ready_act"), 3)
            for n in range(8):
                c, q = divmod(n, 4)
                last = pe.transpose(PS[:, 7, n * ROW:(n + 1) * ROW], a_["RQ"][0:ROW, q, c * P:(c + 1) * P],
                                    IDENT[0:ROW, 0:ROW])
            last.then_inc(sem("cols_turned"), 1)
            token_product(U_O, 2, "o_free")

            pe.wait_ge(sem("o_free"), 4 + 8)
            with pe.Fori(0, HEADS_A) as h:
                HQ, VA = a_["HQ"], a_["VA"]
                pe.wait_ge(sem("hq_staged"), h + 1)
                pe.matmul(PS[:, 1, :], ONES[0:ROW, :], a_["RSEL"][0:ROW, :, :], start=True, stop=True)\
                    .then_inc(sem("r_spread"), 1)
                for c in range(2):
                    last = pe.transpose(PS[:, 2, c * P:(c + 1) * P], HQ[:, 1, c * P:(c + 1) * P], IDENT)
                last.then_inc(sem("k_turned"), 1)
                for c in range(2):
                    last = pe.matmul(PS[:, 0, c * P:(c + 1) * P], HQ[:, 1, c * P:(c + 1) * P],
                                     HQ[:, 0, c * P:(c + 1) * P], start=True, stop=True)
                last.then_inc(sem("scores_a"), 1)
                pe.wait_ge(sem("kw_ready"), h + 1)
                for d in range(2):
                    last = pe.matmul(PS[:, 3 + d, 0:DV_A + 1], a_["KW"][:, d, :], VA[:, d, h, 0:DV_A + 1],
                                     start=True, stop=True)
                last.then_inc(sem("state_done"), 1)
                pe.wait_ge(sem("state_ready"), h + 1)
                for d in range(2):
                    c = 1 - d
                    last = pe.matmul(PS[:, 3 + d, 0:DV_A + 1], HQ[:, 0, c * P:(c + 1) * P],
                                     a_["CS"][:, d, 0:DV_A + 1], start=True, stop=True)
                last.then_inc(sem("inter_done"), 1)
                pe.wait_ge(sem("dt_ready"), h + 1)
                for j, bank in enumerate((5, 6, 7, 2)):
                    d, c = divmod(j, 2)
                    pe.matmul(PS[:, bank, 0:DV_A + 1], a_["DT"][:, d, c * P:(c + 1) * P], VA[:, c, h, 0:DV_A + 1],
                              start=True, stop=True).then_inc(sem("intra_done"), 1)
            transposes("h")
            xt_ready("h")
            token_product(U_AOUT, 2, "aout_free")

            def route(l):
                xt_ready(f"n{2 * l + 1}")
                pe.wait_ge(sem("router_loaded"), 32)
                for t in range(NT):
                    for k in range(DC):
                        last = pe.matmul(PS[:, 0, t * N_EXP:(t + 1) * N_EXP], XT[:, k, t * P:(t + 1) * P],
                                         RW[:, k, :], start=(k == 0), stop=(k == DC - 1))
                last.then_inc(sem("logits"), 1)
                pe.wait_ge(sem("mask_ready"), l + 1)
                MK = m_["MK"]
                pe.matmul(PS[:, 1, 0:N_EXP], TRI, MK[:, 0, :], start=True, stop=True)
                pe.matmul(PS[:, 1, N_EXP:2 * N_EXP], ONES, MK[:, 0, :], start=True, stop=False)
                pe.matmul(PS[:, 1, N_EXP:2 * N_EXP], TRI, MK[:, 1, :], start=False, stop=True)
                pe.matmul(PS[:, 1, 2 * N_EXP:3 * N_EXP], ONES, MK[:, 0, :], start=True, stop=False)
                pe.matmul(PS[:, 1, 2 * N_EXP:3 * N_EXP], ONES, MK[:, 1, :], start=False, stop=True)\
                    .then_inc(sem("positions"), 1)

            def experts(l, base):
                def gather(m, j):
                    pe.wait_ge(sem(m + "sel_ready"), j + 1)
                    for g in range(4):
                        bank = 2 + g % 2
                        if g >= 2:
                            pe.wait_ge(sem(m + "xg_ready"), 4 * j + g - 1)
                        for k in range(4):
                            c = 4 * g + k
                            for t in range(NT):
                                last = pe.matmul(PS[:, bank, k * P:(k + 1) * P], XN[:, t, c * P:(c + 1) * P],
                                                 m_["SEL"][:, t, :], start=(t == 0), stop=(t == NT - 1))
                        last.then_inc(sem(m + "gathered"), 1)

                def pair(m, j, arrived, slot, consumed, following):
                    pe.wait_ge(sem(m + "xg_ready"), 4 * j + 4)
                    for q in range(4):
                        for n in range(4):
                            arrived(4 * q + n)
                        for kk in range(UNIT_K):
                            k = UNIT_K * q + kk
                            for up in range(2):
                                for e in range(2):
                                    n = 4 * q + 2 * up + e
                                    last = pe.matmul(PS[64 * e:64 * e + 64, up, :], m_["XG"][:, k, 64 * e:64 * e + 64],
                                                     slot(n)[:, kk, :], start=(k == 0), stop=(k == DC - 1))
                                    if kk == UNIT_K - 1:
                                        last.then_inc(consumed, 1)
                    if following:
                        gather(m, j + 1)
                    pe.wait_ge(sem(m + "a_ready"), j + 1)
                    for c in range(FC):
                        last = pe.transpose(PS[:, 4, c * P:(c + 1) * P], m_["A"][:, c * P:(c + 1) * P], IDENT)
                    last.then_inc(sem(m + "a_turned"), 1)
                    for t in range(NT):
                        last = pe.transpose(PS[:, 5, t * P:(t + 1) * P], m_["SELG"][:, t, :], IDENT)
                    last.then_inc(sem(m + "sel_turned"), 1)
                    pe.wait_ge(sem(m + "at_ready"), j + 1)

                    def scatter(d):
                        pe.wait_ge(sem(m + "y_ready"), 4 * j + d + 1)
                        for t in range(NT):
                            if d > 0:
                                pe.wait_ge(sem(m + "x_added"), 8 * j + 2 * d + t - 1)
                            pe.matmul(PS[:, 2 + t, :], m_["SCT"][:, t * P:(t + 1) * P], m_["YS"][:, d, :],
                                      start=True, stop=True).then_inc(sem(m + "scattered"), 1)

                    for d in range(4):
                        for e in range(2):
                            arrived(16 + 2 * d + e)
                        for c in range(FC):
                            for e in range(2):
                                last = pe.matmul(PS[64 * e:64 * e + 64, 6 + d % 2, :], m_["AT"][:, c, 64 * e:64 * e + 64],
                                                 slot(16 + 2 * d + e)[:, c, :], start=(c == 0), stop=(c == FC - 1))
                                if c == FC - 1:
                                    last.then_inc(consumed, 1)
                        if d == 0:
                            if following:
                                pe.wait_ge(sem(m + "xg_ready"), 4 * j + 8)
                            pe.wait_ge(sem(m + "sct_ready"), j + 1)
                        else:
                            scatter(d - 1)
                    scatter(3)

                m = "m_"
                gather(m, PAIRS * l)

                def main(i, following):
                    pair(m, i + PAIRS * l, lambda n: unit_arrived(pe, base + n, i, PAIR_UNITS),
                         lambda n: ring[(base + n) % RING], used, following)
                with pe.Fori(0, PAIRS - 1) as i:
                    main(i, True)
                main(PAIRS - 1, False)
                m = f"o{l}_"
                flag = pe.value_load(FLAG[0:1, l:l + 1], min_val=0, max_val=1)
                with pe.If(flag > 0):
                    with pe.Fori(0, EXTRA) as q:
                        with pe.Fori(0, PAIRS) as i:
                            j = q * PAIRS + i
                            gather(m, j)
                            pair(m, j,
                                 lambda n: pe.wait_ge(sem(f"over_loaded_{l}_{n % 4}"),
                                                      16 * (PAIR_UNITS // 4) * j + 16 * (n // 4 + 1)),
                                 lambda n: ov_ring[n % 4], sem(f"over_free_{l}"), False)

            transposes("n1")
            route(0)
            experts(0, U_MOE0)

            transposes("n2")
            xt_ready("n2")
            token_block(U_CKV, 0, 0, "ckv_free", 2)
            pe.wait_ge(sem("wkr_loaded"), 16)
            for t in range(NT):
                for k in range(DC):
                    last = pe.matmul(PS[:, 4, t * ROPE:(t + 1) * ROPE], XT[:, k, t * P:(t + 1) * P],
                                     b_["WKR"][:, k, :], start=(k == 0), stop=(k == DC - 1))
            last.then_inc(sem("krope_done"), 1)
            token_product(U_Q, 3, "q_free")
            pe.wait_ge(sem("ckv_normed"), 2)
            for t in range(NT):
                for c in range(RC):
                    last = pe.transpose(PS[:, 4 + t, c * P:(c + 1) * P], b_["CKV"][:, t, c * P:(c + 1) * P], IDENT)
            last.then_inc(sem("ckv_turned"), 1)
            pe.wait_ge(sem("ckt_ready"), 2)
            for n in range(8):
                unit_arrived(pe, U_UKV + n)
                pe.wait_ge(sem("kv_free"), 2 * n + 2)
                for k in range(RC):
                    for t in range(NT):
                        last = pe.matmul(PS[:, 2 * (n % 2) + t, :], b_["CKT"][:, k, t * P:(t + 1) * P],
                                         ring[(U_UKV + n) % RING][:, k, :], start=(k == 0), stop=(k == RC - 1))
                last.then_inc(used, 1)
            pe.wait_ge(sem("kv_free"), 4 + 16)
            with pe.Fori(0, HEADS_B // 2) as i:
                for p in range(2):
                    h = 2 * i + p
                    pe.wait_ge(sem("qk_normed"), h + 1)
                    pe.wait_ge(sem("o_copied"), 2 * i + 1)
                    for t in range(NT):
                        pe.transpose(PS[:, 4 * p, t * P:(t + 1) * P], QN[p][:, t, 0:NOPE], IDENT)
                        last = pe.transpose(PS[:, 4 * p, SEQ + t * P:SEQ + (t + 1) * P], KN[p][:, t, 0:NOPE], IDENT)
                    last.then_inc(sem("nope_turned"), 1)
                    for t in range(NT):
                        pe.transpose(PS[0:ROPE, 4 * p + 1, t * P:(t + 1) * P], QN[p][:, t, NOPE:DQ_B], IDENT)
                        last = pe.transpose(PS[0:ROPE, 4 * p + 1, SEQ + t * P:SEQ + (t + 1) * P],
                                            KN[p][:, t, NOPE:DQ_B], IDENT)
                    last.then_inc(sem("rope_turned"), 1)
                for p in range(2):
                    h = 2 * i + p
                    pe.wait_ge(sem("nope_ready"), h + 1)
                    pe.wait_ge(sem("rope_ready"), h + 1)
                    for t in range(NT):
                        o = PS[:, 4 * p + 2, t * SEQ:(t + 1) * SEQ]
                        pe.matmul(o, QKN[p][:, t * P:(t + 1) * P], QKN[p][:, SEQ:2 * SEQ], start=True, stop=False)
                        last = pe.matmul(o, QKR[p][0:ROPE, t * P:(t + 1) * P], QKR[p][0:ROPE, SEQ:2 * SEQ],
                                         start=False, stop=True)
                    last.then_inc(sem("scores_b"), 1)
                for p in range(2):
                    h = 2 * i + p
                    pe.wait_ge(sem("probs_ready"), h + 1)
                    for t in range(NT):
                        for s in range(NT):
                            last = pe.transpose(PS[:, 4 * p + 3, s * SEQ + t * P:s * SEQ + (t + 1) * P],
                                                PR[p][:, t, s * P:(s + 1) * P], IDENT)
                    last.then_inc(sem("probs_turned"), 1)
                for p in range(2):
                    h = 2 * i + p
                    pe.wait_ge(sem("pt_ready"), h + 1)
                    for s in range(NT):
                        last = pe.matmul(PS[:, 4 * p, 0:SEQ], VS[p][:, s, :], PT[p][:, s, :],
                                         start=(s == 0), stop=(s == NT - 1))
                    last.then_inc(sem("o_done"), 1)
            pe.wait_ge(sem("o_copied"), HEADS_B + 1)
            token_product(U_BOUT, 2, "bout_free")
            transposes("n3")
            route(1)
            experts(1, U_MOE1)

        @block.scalar
        def _(act):
            load = act.dma_start
            load(X[:, :, :], w["x"].rearrange("b (t p) d -> p (b t) d", p=P)).then_inc(sem("x_ready"), 16)
            load(ROWS[V_MIX:V_MIX + 32, :], w["norm_mix"].rearrange("l (c p) -> (l c) p", p=P)).then_inc(sem("vectors_loaded"), 16)
            load(ROWS[V_FFN:V_FFN + 32, :], w["norm_ffn"].rearrange("l (c p) -> (l c) p", p=P)).then_inc(sem("vectors_loaded"), 16)
            load(ROWS[V_CONV:V_CONV + 48, :], w["a_conv_w"].rearrange("a k (c p) -> (a k c) p", p=P)).then_inc(sem("vectors_loaded"), 16)
            load(ROWS[V_KV:V_KV + 4, :], w["b_kv_norm"].rearrange("a (c p) -> (a c) p", p=P)).then_inc(sem("vectors_loaded"), 16)
            load(ROWS2[:, :], w["a_out_norm"].rearrange("a (c p) -> (a c) p", p=P)).then_inc(sem("vectors_loaded"), 16)
            load(a_["GB"], w["a_gate_b"].broadcast_to([P, N_GATES])).then_inc(sem("vectors_loaded"), 16)
            load(CON[:, :], w["consts"]).then_inc(sem("consts_loaded"), 16)
            load(a_["WG"], w["a_w_in"][0].rearrange("(c p) n -> p c n", p=P)[:, :, QK_CH + 2 * D:]).then_inc(sem("wg_loaded"), 16)
            load(RW[:, :, :], w["router_w"].rearrange("(c p) n -> p c n", p=P)).then_inc(sem("router_loaded"), 16)
            load(RB[:, :], w["router_b"].rearrange("(a n) -> a n", a=1).broadcast_to([P, N_EXP])).then_inc(sem("router_loaded"), 16)

            def norm(tag, junk):
                at = NORMS.index(tag)
                act.wait_ge(sem("x_ready"), 16 + at)
                for t in range(NT):
                    if t:
                        act.wait_ge(sem("squares"), NT * at + t)
                    act.activation(junk, X[:, t, :], ACT.Square, accum_out=SSQ[:, t:t + 1]).then_inc(sem("squares"), 1)
                act.wait_ge(sem("means"), at + 1)
                act.activation(SSQ[:, 4:6], SSQ[:, 2:4], ACT.Sqrt).then_inc(sem("roots"), 1)

            norm("n0", a_["JUNK"])
            act.wait_ge(sem("pads_zeroed"), 1)
            act.drain().then_inc(sem("qk_free"), 8)
            with act.Fori(0, 2) as i:
                for n in range(8):
                    cc = 8 * i + n
                    act.wait_ge(sem("unit_used"), U_QK + 8 * i + 4 * (n // 4) + 4)
                    act.wait_ge(sem("conv_done"), cc + 1)
                    act.activation(a_["PAD"][:, n % 2, 1:SEQ + 1], PS[:, n, 0:SEQ], ACT.Copy).then_inc(sem("qk_free"), 1)
                    act.wait_ge(sem("conv_done"), cc + 3)
                    act.activation(a_["SGC"][:, n % 2, :], a_["CT"][:, n % 2, :], ACT.Sigmoid).then_inc(sem("conv_sig"), 1)
            act.wait_ge(sem("abs_ready"), 1)
            act.activation(a_["T1"][0:ROW, :], a_["T1"][0:ROW, :], ACT.Exp, scale=-1.0).then_inc(sem("gate_exp"), 1)
            act.wait_ge(sem("gate_exp"), 1)
            act.activation(a_["T1"][0:ROW, :], a_["T1"][0:ROW, :], ACT.Ln, bias=1.0).then_inc(sem("gate_ln"), 1)
            act.drain().then_inc(sem("v_free"), 4)
            act.wait_ge(sem("scans_done"), 1)
            RQ, R, MP = a_["RQ"], a_["R"], a_["MP"]
            for d in range(2):
                rows = slice(0, 32) if d == 0 else slice(32, ROW)
                c1, c2 = (0, 1) if d == 0 else (1, 0)
                act.activation(RQ[rows, 1, c2 * P:(c2 + 1) * P], R[rows, c2 * P:(c2 + 1) * P], ACT.Exp,
                               bias=MP[rows, 0:1], scale=-1.0)
                last = act.activation(RQ[rows, 3, c1 * P:(c1 + 1) * P], RQ[rows, 0, c1 * P:(c1 + 1) * P], ACT.Exp,
                                      bias=MP[rows, 1:2])
                last.then_inc(sem("rows_ready_act"), 1)
            act.activation(RQ[0:ROW, 2, :], a_["T2"][0:ROW, :], ACT.Exp, scale=-1.0).then_inc(sem("rows_ready_act"), 1)

            with act.Fori(0, 2) as i:
                for b in range(2):
                    act.wait_ge(sem("unit_used"), U_V + 8 * i + 4 * b + 4)
                    for t in range(NT):
                        act.activation(a_["VA"][:, t, ds(4 * i + 2 * b, 2), 0:DV_A],
                                       PS[:, 2 * b + t, :].rearrange("p (a b) -> p a b", a=2), ACT.Copy)\
                            .then_inc(sem("v_free"), 1)
            act.drain().then_inc(sem("o_free"), 4)
            with act.Fori(0, 2) as i:
                for b in range(2):
                    act.wait_ge(sem("unit_used"), U_O + 8 * i + 4 * b + 4)
                    for t in range(NT):
                        act.activation(a_["OG"][:, t, ds(UNIT_C * (2 * i + b), UNIT_C)], PS[:, 2 * b + t, :], ACT.Sigmoid)\
                            .then_inc(sem("o_free"), 1)

            with act.Fori(0, HEADS_A) as h:
                act.wait_ge(sem("k_turned"), h + 1)
                for d in range(2):
                    last = act.activation(a_["KW"][:, d, :], PS[:, 2, d * P:(d + 1) * P], ACT.Copy,
                                          scale=a_["COLT"][:, 4 * d + 3, ds(h + 32 * d, 1)])
                last.then_inc(sem("kw_ready"), 1)
                act.wait_ge(sem("z_ready"), h + 1)
                act.activation(a_["Z"], a_["Z"], ACT.Exp, scale=-1.0).then_inc(sem("decay_ready"), 1)
                act.wait_ge(sem("state_done"), h + 1)
                for d in range(2):
                    last = act.activation(a_["CS"][:, d, 0:DV_A + 1], PS[:, 3 + d, 0:DV_A + 1], ACT.Copy)
                last.then_inc(sem("state_ready"), 1)
                for j, bank in enumerate((5, 6, 7, 2)):
                    act.wait_ge(sem("intra_done"), 4 * h + j + 1)
                    act.activation(a_["NS"][:, j, 0:DV_A + 1], PS[:, bank, 0:DV_A + 1], ACT.Copy)\
                        .then_inc(sem("intra_ready"), 1)
            act.wait_ge(sem("head_sums"), 1)
            act.activation(SMA[:, 1, :], SMA[:, 0, :], ACT.Sqrt).then_inc(sem("head_roots"), 1)

            def experts(l, base):
                act.wait_ge(sem("logits"), l + 1)
                act.activation(m_["SC"], PS[:, 0, 0:NT * N_EXP].rearrange("p (t e) -> p t e", t=NT), ACT.Sigmoid)\
                    .then_inc(sem("scores"), 1)

                def pair(m, j, products):
                    products(16)
                    act.activation(m_["SIG"], PS[:, 0, :], ACT.Sigmoid).then_inc(sem(m + "sig"), 1)
                    act.wait_ge(sem(m + "a_turned"), j + 1)
                    act.activation(m_["AT"], ps4(4), ACT.Copy).then_inc(sem(m + "at_ready"), 1)
                    for d in range(4):
                        products(16 + 2 * (d + 1))
                        act.activation(m_["YS"][:, d, :], PS[:, 6 + d % 2, :], ACT.Copy).then_inc(sem(m + "y_ready"), 1)

                with act.Fori(0, PAIRS) as i:
                    pair("m_", i + PAIRS * l, lambda n: act.wait_ge(sem("unit_used"), base + PAIR_UNITS * i + n))
                flag = act.value_load(FLAG[0:1, l:l + 1], min_val=0, max_val=1)
                with act.If(flag > 0):
                    with act.Fori(0, EXTRA) as q:
                        with act.Fori(0, PAIRS) as i:
                            j = q * PAIRS + i
                            pair(f"o{l}_", j, lambda n: act.wait_ge(sem(f"over_free_{l}"), 4 + PAIR_UNITS * j + n))

            norm("n1", m_["JUNK"])
            experts(0, U_MOE0)

            norm("n2", b_["JUNK"])
            load(b_["WKR"], w["b_w_in"][0].rearrange("(c p) n -> p c n", p=P)[:, :, Q_COLS + RANK:]).then_inc(sem("wkr_loaded"), 16)
            load(b_["QG"], w["b_q_norm"].broadcast_to([P, DQ_B])).then_inc(sem("qk_gains"), 16)
            load(b_["KG"], w["b_k_norm"].broadcast_to([P, DQ_B])).then_inc(sem("qk_gains"), 16)
            act.wait_ge(sem("unit_used"), U_CKV + 4)
            for t in range(NT):
                act.activation(b_["CKV"][:, t, :], PS[:, t, :], ACT.Copy).then_inc(sem("ckv_copied"), 1)
            act.wait_ge(sem("krope_done"), 1)
            act.activation(b_["KR"], PS[:, 4, 0:NT * ROPE].rearrange("p (t r) -> p t r", t=NT), ACT.Copy)\
                .then_inc(sem("krope_copied"), 1)
            act.drain().then_inc(sem("q_free"), 4)
            act.wait_ge(sem("ckv_means"), 1)
            act.activation(SSQ[:, 4:6], SSQ[:, 2:4], ACT.Sqrt).then_inc(sem("ckv_roots"), 1)
            with act.Fori(0, 3) as i:
                for b in range(2):
                    act.wait_ge(sem("unit_used"), U_Q + 8 * i + 4 * b + 4)
                    for t in range(NT):
                        act.activation(b_["Q"][:, t, ds(UNIT_C * (2 * i + b), UNIT_C)], PS[:, 2 * b + t, :], ACT.Copy)\
                            .then_inc(sem("q_free"), 1)
            act.drain().then_inc(sem("kv_free"), 4)
            for n in range(8):
                act.wait_ge(sem("unit_used"), U_UKV + n + 1)
                for t in range(NT):
                    act.activation(b_["KV"][:, t, n * UNIT_C:(n + 1) * UNIT_C], PS[:, 2 * (n % 2) + t, :], ACT.Copy)\
                        .then_inc(sem("kv_free"), 1)
            act.wait_ge(sem("qk_means"), 1)
            act.activation(b_["SS"], b_["SS"], ACT.Sqrt).then_inc(sem("qk_roots"), 1)
            act.drain().then_inc(sem("o_copied"), 1)
            with act.Fori(0, HEADS_B // 2) as i:
                for p in range(2):
                    h = 2 * i + p
                    act.wait_ge(sem("nope_turned"), h + 1)
                    act.activation(QKN[p], PS[:, 4 * p, :], ACT.Copy).then_inc(sem("nope_ready"), 1)
                    act.wait_ge(sem("rope_turned"), h + 1)
                    act.activation(QKR[p][0:ROPE, :], PS[0:ROPE, 4 * p + 1, :], ACT.Copy).then_inc(sem("rope_ready"), 1)
                for p in range(2):
                    h = 2 * i + p
                    act.wait_ge(sem("max_ready"), h + 1)
                    for t in range(NT):
                        act.activation(PR[p][:, t, :], PS[:, 4 * p + 2, t * SEQ:(t + 1) * SEQ], ACT.Exp,
                                       bias=SM[:, p, t:t + 1], accum_out=SM[:, p, 2 + t:3 + t]).then_inc(sem("exp_done"), 1)
                for p in range(2):
                    h = 2 * i + p
                    act.wait_ge(sem("probs_turned"), h + 1)
                    act.activation(PT[p], PS[:, 4 * p + 3, :].rearrange("p (a b) -> p a b", a=2), ACT.Copy)\
                        .then_inc(sem("pt_ready"), 1)
                for p in range(2):
                    h = 2 * i + p
                    act.wait_ge(sem("o_done"), h + 1)
                    act.activation(XT[:, ds(h, 1), :], PS[:, 4 * p, 0:SEQ].unsqueeze(1), ACT.Copy).then_inc(sem("o_copied"), 1)
            norm("n3", m_["JUNK"])
            experts(1, U_MOE1)

        @block.vector
        def _(dve):
            tt, ts, stt, red = dve.tensor_tensor, dve.tensor_scalar, dve.scalar_tensor_tensor, dve.tensor_reduce

            dve.wait_ge(sem("vectors_turned"), 1)
            dve.tensor_copy(VEC[:, 0:V_ROWS], PS[:, 7, 0:V_ROWS]).then_inc(sem("vec_ready"), 1)
            dve.tensor_copy(VEC[:, V_OUT:V_ALL], PS[:, 7, 128:144]).then_inc(sem("vec_ready"), 1)
            dve.wait_ge(sem("vec_ready"), 2)

            link = Chain(dve, sem("vector_chain"))

            def norm(tag):
                at = NORMS.index(tag)
                dve.wait_ge(sem("squares"), NT * (at + 1))
                ts(SSQ[:, 2:4], SSQ[:, 0:2], 1.0 / D, EPS, ALU.mult, ALU.add).then_inc(sem("means"), 1)
                dve.wait_ge(sem("roots"), at + 1)
                link(dve.reciprocal(SSQ[:, 6:8], SSQ[:, 4:6]))
                for t in range(NT):
                    ts(XN[:, t, :], X[:, t, :], SSQ[:, 6 + t:7 + t], None, ALU.mult).then_inc(sem("xn_ready"), 1)

            def turned(tag, gain):
                for n in range(8):
                    t, g = divmod(n, 4)
                    dve.wait_ge(sem("turned"), 8 * TURNS.index(tag) + n + 1)
                    tt(XT[:, 4 * g:4 * g + 4, t * P:(t + 1) * P], ps4(n), vec4(gain + 4 * g), ALU.mult)\
                        .then_inc(sem("xt_ready"), 1)

            norm("n0")
            turned("n0", V_MIX)

            GP = a_["GP"]
            dve.memset(GP, 0.0).then_inc(sem("gp_zeroed"), 1)
            dve.wait_ge(sem("gp_zeroed"), 1)
            dve.wait_ge(sem("gates_done"), 1)
            for d in range(2):
                for t in range(NT):
                    g0 = 16 * d
                    last = tt(GP[:, :, :].rearrange("p (y t) r -> p t y r", t=2)[:, t, :, 32 * d:32 * d + 8],
                              PS[:, 7, t * N_GATES + g0:t * N_GATES + g0 + 16].rearrange("p (y h) -> p y h", y=2),
                              a_["GB"][:, g0:g0 + 16].rearrange("p (y h) -> p y h", y=2), ALU.add)
                last.then_inc(sem("gates_read"), 1)
            dve.memset(a_["PAD"], 0.0).then_inc(sem("pads_zeroed"), 1)
            dve.memset(a_["VA"][:, :, :, DV_A:VW], 1.0)
            dve.drain().then_inc(sem("conv_done"), 2)
            with dve.Fori(0, 2) as i:
                step = Chain(dve, sem("chain_conv"), 16 * i)
                PAD, CT, SGC = a_["PAD"], a_["CT"], a_["SGC"]
                for n in range(8):
                    p, cc = n % 2, 8 * i + n
                    dve.wait_ge(sem("qk_free"), 8 + cc + 1)
                    step(ts(CT[:, p, :], PAD[:, p, 1:SEQ + 1], vec(V_CONV + 16 + cc), None, ALU.mult))
                    step(stt(CT[:, p, :], PAD[:, p, 0:SEQ], vec(V_CONV + cc), CT[:, p, :], ALU.mult, ALU.add))
                    stt(CT[:, p, :], PAD[:, p, 2:SEQ + 2], vec(V_CONV + 32 + cc), CT[:, p, :], ALU.mult, ALU.add)\
                        .then_inc(sem("conv_done"), 1)
                    dve.wait_ge(sem("conv_sig"), cc + 1)
                    tt(a_["QKT"][:, ds(cc, 1), :], CT[:, p:p + 1, :], SGC[:, p:p + 1, :], ALU.mult)\
                        .then_inc(sem("qk_ready"), 1)

            LI, LF, T1, T2, B, R, RQ, MP = (a_[n] for n in ("LI", "LF", "T1", "T2", "B", "R", "RQ", "MP"))
            dve.wait_ge(sem("gate_rows"), 1)
            dve.tensor_copy(LI[0:ROW, :], PS[0:ROW, 6, 0:SEQ])
            dve.memset(RQ[0:ROW, :, :], 0.0)
            link(dve.tensor_copy(LF[0:ROW, :], PS[0:ROW, 6, SEQ:2 * SEQ]))
            stt(T1[0:ROW, :], LF[0:ROW, :], -1.0, LF[0:ROW, :], ALU.mult, ALU.max).then_inc(sem("abs_ready"), 1)
            link(ts(LF[0:ROW, :], LF[0:ROW, :], 0.0, None, ALU.min))
            dve.wait_ge(sem("gate_ln"), 1)
            link(tt(LF[0:ROW, :], LF[0:ROW, :], T1[0:ROW, :], ALU.subtract))

            def span(v, d, c):
                rows = slice(0, 32) if d == 0 else slice(32, ROW)
                s = v[rows, c * P:(c + 1) * P]
                return s if d == 0 else s[:, ::-1]

            def one(v, d, at):
                rows = slice(0, 32) if d == 0 else slice(32, ROW)
                return v[rows, at:at + 1]

            for d in range(2):
                for c in range(2):
                    last = dve.tensor_tensor_scan(span(B, d, c), span(CON[:, C_ONE:C_ONE + SEQ], d, 0), span(LF, d, c), 0.0,
                                                  ALU.mult, ALU.add)
            link(last)
            link(tt(RQ[0:ROW, 0, :], LI[0:ROW, :], B[0:ROW, :], ALU.subtract))
            for d in range(2):
                c1 = d
                last = dve.tensor_tensor_scan(span(R, d, c1), span(CON[:, C_ONE:C_ONE + SEQ], d, 0),
                                              span(RQ[:, 0, :], d, c1), 0.0, ALU.mult, ALU.max)
            link(last)
            for d, at in ((0, P - 1), (1, P)):
                tt(one(MP, d, 0), one(B, d, at), one(R, d, at), ALU.add)
                last = ts(one(MP, d, 1), one(R, d, at), -1.0, None, ALU.mult)
            link(last)
            for d in range(2):
                c2 = 1 - d
                last = dve.tensor_tensor_scan(span(R, d, c2), span(CON[:, C_ONE:C_ONE + SEQ], d, 0),
                                              span(RQ[:, 0, :], d, c2), one(MP, d, 0), ALU.mult, ALU.max)
            link(last)
            link(tt(T2[0:ROW, :], B[0:ROW, :], R[0:ROW, :], ALU.add))
            dve.drain().then_inc(sem("scans_done"), 1)
            dve.drain().then_inc(sem("rows_ready"), 1)
            dve.wait_ge(sem("cols_turned"), 1)
            COLT = a_["COLT"]
            link(dve.tensor_copy(COLT, PS[:, 7, 0:8 * ROW].rearrange("p (a b) -> p a b", b=ROW)))

            dve.wait_ge(sem("qk_ready"), 16)
            n_links = 7
            with dve.Fori(0, HEADS_A) as h:
                step = Chain(dve, sem("chain_heads"), n_links * h)
                HQ, RSEL, Z, NS, DEN = (a_[n] for n in ("HQ", "RSEL", "Z", "NS", "DEN"))
                ts(HQ[:, 0:1, :], a_["QKT"][:, ds(h, 1), :], DQK_A ** -0.5, None, ALU.mult)
                dve.tensor_copy(HQ[:, 1:2, :], a_["QKT"][:, ds(h + 8, 1), :])
                for d in range(2):
                    last = ts(RSEL[0:ROW, d, :], R[0:ROW, :], CON[0:ROW, ds(C_ID + 32 * d + h, 1)], None, ALU.mult)
                last.then_inc(sem("hq_staged"), 1)
                dve.wait_ge(sem("r_spread"), h + 1)
                for d in range(2):
                    for c in range(2):
                        last = stt(Z[:, d, c * P:(c + 1) * P], PS[:, 1, d * SEQ + c * P:d * SEQ + (c + 1) * P],
                                   COLT[:, 4 * c, ds(h + 32 * d, 1)], CON[:, C_MASK + d * P:C_MASK + (d + 1) * P],
                                   ALU.subtract, ALU.add)
                last.then_inc(sem("z_ready"), 1)
                dve.wait_ge(sem("decay_ready"), h + 1)
                dve.wait_ge(sem("scores_a"), h + 1)
                tt(a_["DT"], Z, PS[:, 0:1, 0:SEQ].broadcast_to([P, 2, SEQ]), ALU.mult).then_inc(sem("dt_ready"), 1)
                dve.wait_ge(sem("inter_done"), h + 1)
                dve.wait_ge(sem("intra_ready"), 4 * h + 4)
                for d in range(2):
                    c = 1 - d
                    j = 2 * d + c
                    last = stt(NS[:, j, 0:DV_A + 1], PS[:, 3 + d, 0:DV_A + 1], COLT[:, 4 * c + 1, ds(h + 32 * d, 1)],
                               NS[:, j, 0:DV_A + 1], ALU.mult, ALU.add)
                step(last)
                den = NS[:, :, DV_A:DV_A + 1]
                step(stt(DEN[:, 0:4].unsqueeze(2), den, -1.0, den, ALU.mult, ALU.max))
                for j in range(4):
                    d, c = divmod(j, 2)
                    last = ts(DEN[:, j:j + 1], DEN[:, j:j + 1], COLT[:, 4 * c + 2, ds(h + 32 * d, 1)], None, ALU.max)
                step(last)
                step(dve.reciprocal(DEN[:, 4:8], DEN[:, 0:4]))
                for c in range(2):
                    last = ts(NS[:, c, 0:DV_A], NS[:, c, 0:DV_A], DEN[:, 4 + c:5 + c], None, ALU.mult)
                step(last)
                for c in range(2):
                    last = stt(NS[:, c, 0:DV_A], NS[:, 2 + c, 0:DV_A], DEN[:, 6 + c:7 + c], NS[:, c, 0:DV_A],
                               ALU.mult, ALU.add)
                step(last)
                step(dve.tensor_copy(XN[:, :, ds(DV_A * h, DV_A)], NS[:, 0:2, 0:DV_A]))
                assert step.n == n_links
            for t in range(NT):
                link(tt(a_["JUNK"], XN[:, t, :], XN[:, t, :], ALU.mult))
                link(red(SMA[:, 0, 8 * t:8 * t + 8], a_["JUNK"].rearrange("p (h v) -> p h v", h=HEADS_A), AX.X, ALU.add))
            ts(SMA[:, 0, :], SMA[:, 0, :], 1.0 / DV_A, EPS, ALU.mult, ALU.add).then_inc(sem("head_sums"), 1)
            dve.wait_ge(sem("head_roots"), 1)
            link(dve.reciprocal(SMA[:, 1, :], SMA[:, 1, :]))
            for t in range(NT):
                xh = XN[:, t, :].rearrange("p (h v) -> p h v", h=HEADS_A)
                link(tt(xh, xh, SMA[:, 1, 8 * t:8 * t + 8].unsqueeze(2).broadcast_to([P, HEADS_A, DV_A]), ALU.mult))
                tt(XN[:, t, :], XN[:, t, :], a_["OG"][:, t, :], ALU.mult).then_inc(sem("xn_ready"), 1)
            turned("h", V_OUT)

            def residual(base, free, done):
                dve.drain().then_inc(sem(free), 4)
                with dve.Fori(0, 2) as i:
                    for b in range(2):
                        dve.wait_ge(sem("unit_used"), base + 8 * i + 4 * b + 4)
                        for t in range(NT):
                            xs = X[:, t, ds(UNIT_C * (2 * i + b), UNIT_C)]
                            tt(xs, PS[:, 2 * b + t, :], xs, ALU.add).then_inc(sem(free), 1)
                dve.drain().then_inc(sem(done), 1)

            def route(l):
                SC, SR, MK, GATE, KEY = (m_[n] for n in ("SC", "SR", "MK", "GATE", "KEY"))
                G1, G2, G3, G4, G5, G6 = (m_[f"G{n}"] for n in range(1, 7))
                dve.wait_ge(sem("router_loaded"), 32)
                dve.wait_ge(sem("scores"), l + 1)
                link(tt(SR, SC, RB[:, :].unsqueeze(1).broadcast_to([P, NT, N_EXP]), ALU.add))
                lt = CON[:, C_LT:C_LT + 16].rearrange("p (j i) -> p j i", j=4)
                full = [P, N_GRP, 4, 4]
                for t in range(NT):
                    s = SR[:, t, :].rearrange("p (g e) -> p g e", g=N_GRP)
                    g1, g2 = (g.rearrange("p (g j i) -> p g j i", g=4, j=4) for g in (G1, G2))
                    si, sj = s.unsqueeze(2).broadcast_to(full), s.unsqueeze(3).broadcast_to(full)
                    tt(g1, si, sj, ALU.is_gt)
                    link(tt(g2, si, sj, ALU.is_equal))
                    link(tt(g2, g2, lt.unsqueeze(1).broadcast_to(full), ALU.mult))
                    link(tt(G1, G1, G2, ALU.add))
                    link(red(G3, G1.rearrange("p (a i) -> p a i", i=4), AX.X, ALU.add))
                    link(ts(G4, G3, 1.5, None, ALU.is_lt))
                    link(tt(G5, G4, SR[:, t, :], ALU.mult))
                    link(red(G6[:, 0:4], G5.rearrange("p (a i) -> p a i", i=4), AX.X, ALU.add))
                    gs = G6[:, 0:4]
                    h1, h2 = (g[:, 0:16].rearrange("p (j i) -> p j i", j=4) for g in (G1, G2))
                    gi, gj = gs.unsqueeze(1).broadcast_to([P, 4, 4]), gs.unsqueeze(2).broadcast_to([P, 4, 4])
                    tt(h1, gi, gj, ALU.is_gt)
                    link(tt(h2, gi, gj, ALU.is_equal))
                    link(tt(h2, h2, lt, ALU.mult))
                    link(tt(h1, h1, h2, ALU.add))
                    link(red(G6[:, 4:8], h1, AX.X, ALU.add))
                    link(ts(G6[:, 8:12], G6[:, 4:8], 0.5, None, ALU.is_lt))
                    mk = MK[:, t, :].rearrange("p (g e) -> p g e", g=4)
                    link(tt(mk, G4.rearrange("p (g e) -> p g e", g=4),
                            G6[:, 8:12].unsqueeze(2).broadcast_to([P, 4, 4]), ALU.mult))
                    link(tt(GATE[:, t, :], MK[:, t, :], SC[:, t, :], ALU.mult))
                    link(red(G5[:, 0:1], GATE[:, t, :], AX.X, ALU.add))
                    link(dve.reciprocal(G5[:, 1:2], G5[:, 0:1]))
                    link(ts(GATE[:, t, :], GATE[:, t, :], G5[:, 1:2], None, ALU.mult))
                dve.drain().then_inc(sem("mask_ready"), 1)
                dve.wait_ge(sem("positions"), l + 1)
                pos = PS[:, 1, 0:NT * N_EXP].rearrange("p (t e) -> p t e", t=NT)
                red(G5[:, 2:3], PS[:, 1, NT * N_EXP:3 * N_EXP], AX.X, ALU.max)
                link(stt(KEY, pos, 1.0, MK, ALU.add, ALU.mult))
                link(ts(KEY, KEY, -1.0, None, ALU.add))
                ts(FLAG[:, l:l + 1], G5[:, 2:3], float(SLOTS), None, ALU.is_gt).then_inc(sem("routed"), 1)
                dve.wait_ge(sem("routed"), l + 1)

            def experts(l, gain, done):
                SEL, SELG, KEY, GATE = m_["SEL"], m_["SELG"], m_["KEY"], m_["GATE"]

                def select(m, j, i, first):
                    for t in range(NT):
                        for e in range(2):
                            last = ts(SEL[:, t, SLOTS * e:SLOTS * (e + 1)], CON[:, ds(C_IOTA + first, SLOTS)],
                                      KEY[:, t, ds(2 * i + e, 1)], None, ALU.is_equal)
                    last.then_inc(sem(m + "sel_ready"), 1)

                def select_gated(m, j, i, first):
                    for t in range(NT):
                        for e in range(2):
                            last = ts(SELG[:, t, SLOTS * e:SLOTS * (e + 1)], CON[:, ds(C_IOTA + first, SLOTS)],
                                      KEY[:, t, ds(2 * i + e, 1)], GATE[:, t, ds(2 * i + e, 1)], ALU.is_equal, ALU.mult)
                    last.then_inc(sem(m + "selg_ready"), 1)

                def gathered(m, j):
                    for g in range(4):
                        dve.wait_ge(sem(m + "gathered"), 4 * j + g + 1)
                        tt(m_["XG"][:, 4 * g:4 * g + 4, :], ps4(2 + g % 2), vec4(gain + 4 * g), ALU.mult)\
                            .then_inc(sem(m + "xg_ready"), 1)

                def pair(m, j, following, i, first):
                    if following:
                        select(m, j + 1, i + 1, first)
                    select_gated(m, j, i, first)
                    dve.wait_ge(sem(m + "sig"), j + 1)
                    tt(m_["SIG"], PS[:, 0, :], m_["SIG"], ALU.mult).then_inc(sem(m + "silu"), 1)
                    dve.wait_ge(sem(m + "silu"), j + 1)
                    tt(m_["A"], PS[:, 1, :], m_["SIG"], ALU.mult).then_inc(sem(m + "a_ready"), 1)
                    if following:
                        gathered(m, j + 1)
                    dve.wait_ge(sem(m + "sel_turned"), j + 1)
                    dve.tensor_copy(m_["SCT"], PS[:, 5, 0:SEQ]).then_inc(sem(m + "sct_ready"), 1)
                    for d in range(4):
                        for t in range(NT):
                            dve.wait_ge(sem(m + "scattered"), 8 * j + 2 * d + t + 1)
                            xs = X[:, t, d * UNIT_C:(d + 1) * UNIT_C]
                            tt(xs, PS[:, 2 + t, :], xs, ALU.add).then_inc(sem(m + "x_added"), 1)

                m = "m_"
                first = PAIRS * l
                select(m, first, 0, 0)
                gathered(m, first)
                with dve.Fori(0, PAIRS - 1) as i:
                    pair(m, i + first, True, i, 0)
                pair(m, PAIRS - 1 + first, False, PAIRS - 1, 0)
                m = f"o{l}_"
                flag = dve.value_load(FLAG[0:1, l:l + 1], min_val=0, max_val=1)
                with dve.If(flag > 0):
                    dve.drain().then_inc(sem(f"over_free_{l}"), 4)
                    with dve.Fori(0, EXTRA) as q:
                        with dve.Fori(0, PAIRS) as i:
                            j = q * PAIRS + i
                            first = (q + 1) * SLOTS
                            select(m, j, i, first)
                            gathered(m, j)
                            pair(m, j, False, i, first)
                dve.drain().then_inc(sem(done), 1)

            residual(U_AOUT, "aout_free", "x_ready")
            norm("n1")
            turned("n1", V_FFN)
            route(0)
            experts(0, V_FFN, "x_ready")

            norm("n2")
            turned("n2", V_MIX + 16)
            dve.drain().then_inc(sem("ckv_free"), 2)
            CKV, KR, KRT, KRR, QG, KG, SS, RN = (b_[n] for n in ("CKV", "KR", "KRT", "KRR", "QG", "KG", "SS", "RN"))
            COS = CON[:, C_COS:C_COS + 2 * ROPE].rearrange("p (t r) -> p t r", t=NT)
            SIN = CON[:, C_SIN:C_SIN + 2 * ROPE].rearrange("p (t r) -> p t r", t=NT)

            def swapped(v):
                return v.rearrange("p t (a r) -> p t a r", a=2)[:, :, ::-1, :]

            def halves(v):
                return v.rearrange("p t (a r) -> p t a r", a=2)

            dve.wait_ge(sem("ckv_copied"), 2)
            for t in range(NT):
                link(tt(b_["JUNK"][:, 0:RANK], CKV[:, t, :], CKV[:, t, :], ALU.mult))
                link(red(SSQ[:, t:t + 1], b_["JUNK"][:, 0:RANK], AX.X, ALU.add))
            ts(SSQ[:, 2:4], SSQ[:, 0:2], 1.0 / RANK, EPS, ALU.mult, ALU.add).then_inc(sem("ckv_means"), 1)
            dve.wait_ge(sem("krope_copied"), 1)
            dve.wait_ge(sem("qk_gains"), 32)
            link(tt(KRR, KR, KR, ALU.mult))
            link(red(MPB[:, 0:2], KRR, AX.X, ALU.add))
            link(tt(KR, KR, KG[:, NOPE:DQ_B].unsqueeze(1).broadcast_to([P, NT, ROPE]), ALU.mult))
            link(tt(halves(KRT), swapped(KR), halves(SIN), ALU.mult))
            link(tt(KR, KR, COS, ALU.mult))
            link(tt(KRR, KR, KRT, ALU.add))
            dve.wait_ge(sem("ckv_roots"), 1)
            link(dve.reciprocal(SSQ[:, 6:8], SSQ[:, 4:6]))
            for t in range(NT):
                ts(CKV[:, t, :], CKV[:, t, :], SSQ[:, 6 + t:7 + t], None, ALU.mult).then_inc(sem("ckv_normed"), 1)
            dve.wait_ge(sem("ckv_turned"), 1)
            for t in range(NT):
                tt(b_["CKT"][:, :, t * P:(t + 1) * P], ps4(4 + t), vec4(V_KV), ALU.mult).then_inc(sem("ckt_ready"), 1)
            dve.wait_ge(sem("q_free"), 4 + 12)
            for t in range(NT):
                for part in range(2):
                    n = 8 * DQ_B
                    q = b_["Q"][:, t, part * n:(part + 1) * n]
                    link(tt(b_["JUNK"][:, 0:n], q, q, ALU.mult))
                    link(red(SS[:, t, 8 * part:8 * part + 8], b_["JUNK"][:, 0:n].rearrange("p (h v) -> p h v", v=DQ_B),
                             AX.X, ALU.add))
            dve.wait_ge(sem("kv_free"), 4 + 16)
            for t in range(NT):
                k = b_["KV"][:, t, :].rearrange("p (h v) -> p h v", v=2 * P)[:, :, 0:NOPE]
                j = b_["JUNK"].rearrange("p (h v) -> p h v", v=NOPE)
                link(tt(j, k, k, ALU.mult))
                link(red(SS[:, 2 + t, :], j, AX.X, ALU.add))
                link(ts(SS[:, 2 + t, :], SS[:, 2 + t, :], MPB[:, t:t + 1], None, ALU.add))
            ts(SS, SS, 1.0 / DQ_B, EPS, ALU.mult, ALU.add).then_inc(sem("qk_means"), 1)
            dve.wait_ge(sem("qk_roots"), 1)
            link(dve.reciprocal(RN, SS))
            link(ts(RN[:, 0:2, :], RN[:, 0:2, :], DQ_B ** -0.5, None, ALU.mult))

            per_turn = 6
            with dve.Fori(0, HEADS_B // 2) as i:
                step = Chain(dve, sem("chain_attn"), per_turn * i)
                for p in range(2):
                    h = 2 * i + p
                    q = b_["Q"][:, :, ds(DQ_B * h, DQ_B)]
                    dve.wait_ge(sem("o_copied"), 2 * i + 1)
                    for t in range(NT):
                        stt(QN[p][:, t, :], q[:, t, :], RN[:, t, ds(h, 1)], QG, ALU.mult, ALU.mult)
                        stt(KN[p][:, t, 0:NOPE], b_["KV"][:, t, ds(2 * P * h, NOPE)], RN[:, 2 + t, ds(h, 1)],
                            KG[:, 0:NOPE], ALU.mult, ALU.mult)
                        last = ts(KN[p][:, t, NOPE:DQ_B], KRR[:, t, :], RN[:, 2 + t, ds(h, 1)], None, ALU.mult)
                    dve.tensor_copy(VS[p], b_["KV"][:, :, ds(2 * P * h + NOPE, DV_B)])
                    step(last)
                    qr = QN[p][:, :, NOPE:DQ_B]
                    tt(halves(ROT[p]), swapped(qr), halves(SIN), ALU.mult)
                    step(tt(ROS[p], qr, COS, ALU.mult))
                    tt(qr, ROT[p], ROS[p], ALU.add).then_inc(sem("qk_normed"), 1)
                for p in range(2):
                    h = 2 * i + p
                    dve.wait_ge(sem("scores_b"), h + 1)
                    red(SM[:, p, 0:2], PS[:, 4 * p + 2, :].rearrange("p (t s) -> p t s", t=NT), AX.X, ALU.max,
                        negate=True).then_inc(sem("max_ready"), 1)
                for p in range(2):
                    h = 2 * i + p
                    dve.wait_ge(sem("exp_done"), 2 * h + 2)
                    step(dve.reciprocal(SM[:, p, 4:6], SM[:, p, 2:4]))
                    tt(PR[p], PR[p], SM[:, p, 4:6].unsqueeze(2).broadcast_to([P, NT, SEQ]), ALU.mult)\
                        .then_inc(sem("probs_ready"), 1)
                assert step.n == per_turn

            residual(U_BOUT, "bout_free", "x_ready")
            norm("n3")
            turned("n3", V_FFN + 16)
            route(1)
            experts(1, V_FFN + 16, "x_ready")


_WEIGHTS = ["x", "norm_mix", "norm_ffn", "a_w_in", "a_conv_w", "a_gate_b", "a_out_norm", "a_w_out",
            "b_w_in", "b_kv_norm", "b_w_ukv", "b_q_norm", "b_k_norm", "b_w_out", "router_w", "router_b",
            "moe_w_gate", "moe_w_up", "moe_w_down"]


def constants():
    import numpy as np
    c = np.zeros((P, C_ALL), np.float32)
    p, f = np.arange(P)[:, None], np.arange(P)[None, :]
    c[:, C_ID:C_ID + P] = p == f
    c[:, C_TRI:C_TRI + P] = p < f
    c[:, C_ONE:C_ONE + P] = 1.0
    c[:, C_IOTA:C_IOTA + SEQ] = np.arange(SEQ)
    c[:, C_MASK:C_MASK + P] = np.where(p <= f, 0.0, MASKED)
    c[:, C_MASK + P:C_MASK + 2 * P] = np.where(p >= f, 0.0, MASKED)
    c[:, C_LT:C_LT + 16] = np.array([[i < j for i in range(4)] for j in range(4)]).reshape(-1)
    inv = np.float32(10000.0) ** (-np.arange(HALF, dtype=np.float32) / HALF)
    for t in range(NT):
        ang = (np.arange(P, dtype=np.float32) + t * P)[:, None] * inv[None, :].astype(np.float32)
        cos, sin = np.cos(ang), np.sin(ang)
        c[:, C_COS + t * ROPE:C_COS + (t + 1) * ROPE] = np.concatenate([cos, cos], 1)
        c[:, C_SIN + t * ROPE:C_SIN + (t + 1) * ROPE] = np.concatenate([-sin, sin], 1)
    return c


def kernel(**inputs):
    import numpy as np
    import concourse.bacc as bacc
    from concourse.bass_utils import run_bass_kernel_spmd

    nc = bacc.Bacc("TRN2", target_bir_lowering=False, num_devices=1)
    arrays = {f"in_{n}": np.ascontiguousarray(inputs[n]) for n in _WEIGHTS}
    arrays["in_consts"] = constants()
    w = {n[3:]: nc.dram_tensor(n, a.shape, mybir.dt.float32, kind="ExternalInput").ap() for n, a in arrays.items()}
    out = nc.dram_tensor("out", (1, SEQ, D), mybir.dt.float32, kind="ExternalOutput").ap()
    trunk(nc, w, out)
    r = run_bass_kernel_spmd(nc, [arrays], core_ids=[0])
    return r.results[0]["out"]
```

```python
import concourse.bass as bass
from concourse import mybir
from contextlib import ExitStack

P = 128
D = 2048
SEQ = 256
NT = SEQ // P
DC = D // P
EPS = 1e-6
UNIT_K = 4
UNIT_C = 512
RING = 8

HEADS_A = 8
DV_A = D // HEADS_A
DQK_A = DV_A // 2
QK_CH = 2 * HEADS_A * DQK_A
VW = DV_A + 2
N_GATES = 4 * HEADS_A

HEADS_B = 16
NOPE = 128
ROPE = 64
HALF = ROPE // 2
DQ_B = NOPE + ROPE
DV_B = 128
RANK = 512
RC = RANK // P
Q_COLS = HEADS_B * DQ_B

N_EXP = 16
N_GRP = 4
PER_GRP = N_EXP // N_GRP
F = 512
FC = F // P
PAIRS = N_EXP // 2
SLOTS = 64
EXTRA = SEQ // SLOTS - 1
PAIR_UNITS = 24

C_ID = 0
C_TRI = 128
C_ONE = 256
C_IOTA = 384
C_MASK = 640
C_LT = 896
C_COS = 912
C_SIN = C_COS + 2 * ROPE
C_ALL = C_SIN + 2 * ROPE
MASKED = 1e30

V_MIX = 0
V_FFN = 32
V_CONV = 64
V_KV = 112
V_ROWS = 116
V_OUT = 116
V_ALL = 132

U_QK = 0
U_V = U_QK + 16
U_O = U_V + 16
U_AOUT = U_O + 16
U_MOE0 = U_AOUT + 16
EARLY = range(RING, RING + 6)
U_CKV = U_MOE0 + PAIRS * PAIR_UNITS - len(EARLY)
U_PAIRS = U_CKV + 4
U_BOUT = U_PAIRS + 5 * (HEADS_B // 2)
U_MOE1 = U_BOUT + 16
PAIR_Q = 2 * DQ_B
S_CKV = U_MOE0
S_PAIRS = S_CKV + 4
S_BOUT = S_PAIRS + 5 * (HEADS_B // 2)
S_ALL = S_BOUT + 16
ROW = 40


NORMS = ("n0", "n2")
TURNS = ("n0", "h", "n2")
OUT_BANKS = (((0, 1), (2, 3), (0, 1), (2, 3)), ((6, 7), (0, 1), (2, 3), (0, 1)))


class Chain:

    def __init__(self, eng, sem, base=0):
        self.eng, self.sem, self.base, self.n = eng, sem, base, 0

    def __call__(self, ins):
        self.n += 1
        ins.then_inc(self.sem, 1)
        self.eng.wait_ge(self.sem, self.base + self.n)


def trunk(nc, w, out):
    f32 = mybir.dt.float32
    i32 = mybir.dt.int32
    ALU = mybir.AluOpType
    ACT = mybir.ActivationFunctionType
    AX = mybir.AxisListType
    ds = bass.ds

    ctx = ExitStack()
    with ctx:
        def sb(name, shape, dt=f32):
            return ctx.enter_context(nc.sbuf_tensor(name, shape, dt))

        sems = {}

        def sem(name):
            if name not in sems:
                sems[name] = ctx.enter_context(nc.semaphore(name))
            return sems[name]

        f32r = mybir.dt.float32r
        start = (nc.sbuf_base + 63) // 64 * 64
        top = [start]

        def at(name, offset, shape, dt=f32):
            return nc.alloc_sbuf_tensor_at(name, shape, dt, offset=offset)

        def sb(name, shape, dt=f32):
            n = 4
            for d in shape[1:]:
                n *= d
            offset, top[0] = top[0], top[0] + (n + 31) // 32 * 32
            assert top[0] <= nc.sbuf_usable_end, (name, top[0])
            return at(name, offset, shape, dt)

        X = sb("X", [P, NT, D])
        XN = sb("XN", [P, NT, D])
        XTH = sb("XTH", [P, DC, SEQ], f32r)
        over_at = top[0]
        XTL = sb("XTL", [P, DC, SEQ], f32r)
        HI = [sb(f"HI{s}", [P, UNIT_K, UNIT_C], f32r) for s in range(2)]
        OV = [at(f"OV{s}", over_at + s * UNIT_K * UNIT_C * 4, [P, UNIT_K, UNIT_C]) for s in range(4)]
        EARLY_AT = [at(f"EARLY{s}", over_at - (2 - s) * UNIT_K * UNIT_C * 4, [P, UNIT_K, UNIT_C]) for s in range(2)] + OV
        ring, LO = [], []
        for s in range(RING):
            here = top[0]
            ring.append(sb(f"ring{s}", [P, UNIT_K, UNIT_C]))
            LO.append(at(f"LO{s}", here, [P, UNIT_K, UNIT_C], f32r))
        CON = sb("CON", [P, C_ALL])
        VEC = sb("VEC", [P, V_ALL])
        RW = sb("RW", [P, DC, N_EXP])
        RB = sb("RB", [P, N_EXP])
        SSQ = sb("SSQ", [P, 8])
        FLAG = sb("FLAG", [P, 2], i32)
        SM = sb("SM", [P, 2, 8])
        SMA = sb("SMA", [P, 2, NT * HEADS_A])
        MPB = sb("MPB", [P, NT])
        SSB = sb("SSB", [P, NT, D // UNIT_C])
        PS = ctx.enter_context(nc.psum_tensor("PS", [P, 8, 512], f32))
        IDENT = CON[:, C_ID:C_ID + P]
        TRI = CON[:, C_TRI:C_TRI + P]
        ONES = CON[:, C_ONE:C_ONE + P]

        AREA_W = 13760
        area_at = top[0]
        AREA = sb("AREA", [P, AREA_W])
        WGP = [at(f"WG_{n}", area_at + 4 * a, [P, DC, N_GATES], f32r) for n, a in (("hi", 12704), ("lo", 13216))]
        WKRP = [at(f"WKR_{n}", area_at + 4 * a, [P, DC, ROPE], f32r) for n, a in (("hi", 7712), ("lo", 8736))]
        CKH = at("CKH", area_at + 4 * 11704, [P, RC, SEQ], f32r)
        CKL = at("CKL", area_at + 4 * 12728, [P, RC, SEQ], f32r)

        def carve(whole, limit, sizes):
            at_, views = 0, {}
            for name, shape in sizes:
                n = 1
                for s in shape:
                    n *= s
                v = whole[:, at_:at_ + n]
                if len(shape) == 2:
                    v = v.rearrange("p (a b) -> p a b", a=shape[0])
                if len(shape) == 3:
                    v = v.rearrange("p (a b c) -> p a b c", a=shape[0], b=shape[1])
                views[name] = v
                at_ += n
            assert at_ <= limit, at_
            return views

        XNF = XN[:, :, :].rearrange("p t d -> p (t d)")
        a_ = carve(AREA, AREA_W, [
            ("QKT", (DC, SEQ)), ("VA", (NT, HEADS_A, VW)), ("R", (SEQ,)), ("COLT", (8, ROW)), ("MP", (4,)),
            ("GB", (N_GATES,)), ("RSEL", (2, 2 * SEQ)), ("KW", (2, P)), ("CS", (2, VW)), ("Z", (2, SEQ)),
            ("NS", (4, VW)), ("DEN", (8,)), ("DT", (2, SEQ)), ("OGS", (NT, UNIT_C))])
        a_["WG"] = a_["RSEL"][:, 0, :].rearrange("p (c n) -> p c n", c=DC)
        a_["T"] = AREA[:, AREA_W - 3100:AREA_W - 2076].rearrange("p (a b) -> p a b", a=2)
        a_.update(carve(XNF, 2 * D, [
            ("PAD", (2, SEQ + 2)), ("CT", (2, SEQ)), ("SGC", (2, SEQ)), ("GP", (4, ROW)), ("LI", (SEQ,)),
            ("LF", (SEQ,)), ("T1", (SEQ,)), ("T2", (SEQ,)), ("B", (SEQ,)), ("RQ", (4, SEQ))]))
        b_ = carve(AREA, 11704, [
            ("OT", (DC, SEQ)), ("KVP", (2 * NT, UNIT_C)), ("QP", (NT, PAIR_Q)), ("QG", (DQ_B,)), ("KG", (DQ_B,)),
            ("KR", (NT, ROPE)), ("KRT", (NT, ROPE)), ("KRR", (NT, ROPE)), ("SS", (8,)), ("RT", (8,)), ("RN", (8,)),
            ("HB", (3072,))])
        b_.update(carve(AREA, DC * SEQ, [("CKV", (NT, RANK)), ("WKR", (DC, ROPE)), ("T", (2, 512)), ("JUNK", (RANK,))]))
        HB = [XNF[:, 0:3072], b_["HB"]]
        SQ = XNF[:, 3072:4096]
        m_ = carve(AREA, AREA_W, [
            ("XT", (DC, SEQ)), ("SEL", (2, P)), ("SELG", (2, P)), ("XG", (DC, P)), ("SIG", (F,)), ("A", (F,)),
            ("AT", (FC, P)), ("YS", (4, UNIT_C)), ("SCT", (SEQ,)),
            ("SC", (NT, N_EXP)), ("SR", (NT, N_EXP)), ("MK", (NT, N_EXP)), ("GATE", (NT, N_EXP)),
            ("KEY", (NT, N_EXP)), ("G1", (NT * 4 * N_EXP,)), ("G2", (NT * 4 * N_EXP,)),
            ("G3", (NT * N_EXP,)), ("G4", (NT * N_EXP,)), ("G5", (NT * N_EXP,)), ("G6", (NT * N_EXP,))])
        rows_ = carve(AREA, AREA_W, [("ROWS", (P,)), ("ROWS2", (P,))])
        ROWS, ROWS2 = rows_["ROWS"], rows_["ROWS2"][0:16, :]

        def hb(p, at, shape):
            n = 1
            for s in shape:
                n *= s
            v = HB[p][:, at:at + n]
            return v.rearrange("p (a b) -> p a b", a=shape[0]) if len(shape) == 2 else v

        QN = [hb(p, 0, (2, DQ_B)) for p in range(2)]
        KN = [hb(p, 384, (2, DQ_B)) for p in range(2)]
        ROT = [hb(p, 768, (2, ROPE)) for p in range(2)]
        ROS = [hb(p, 896, (2, ROPE)) for p in range(2)]
        QKN = [hb(p, 1024, (512,)) for p in range(2)]
        QKR = [hb(p, 1536, (512,)) for p in range(2)]
        PR = [hb(p, 2048, (2, SEQ)) for p in range(2)]
        PT = [hb(p, 2560, (2, SEQ)) for p in range(2)]

        def vec(at, n=1):
            return VEC[:, ds(at, n)]

        def vec4(at):
            return VEC[:, at:at + 4].unsqueeze(2).broadcast_to([P, 4, P])

        def ps4(bank):
            return PS[:, bank, :].rearrange("p (a b) -> p a b", a=4)

        def unit_arrived(eng, u, i=0, per=8):
            eng.wait_ge(sem(f"unit_loaded_{u % RING}"), 16 * (u // RING + 1) + 16 * (per // RING) * i)

        def stream(s):
            return s if s < S_CKV else s - S_CKV + U_CKV

        def width(s):
            return PAIR_Q if S_PAIRS <= s < S_BOUT and (s - S_PAIRS) % 5 < 4 else UNIT_C

        block = ctx.enter_context(nc.Block())

        @block.sync
        def _(sp):
            used = sem("unit_used")

            def unit(u, src, i=0, per=8):
                if u >= RING:
                    sp.wait_ge(used, u - RING + 1 + per * i)
                sp.dma_start(ring[u % RING][:, :, 0:src.shape[-1]], src).then_inc(sem(f"unit_loaded_{u % RING}"), 16)

            def matrix(base, view, blocks, first_col):
                def body(i):
                    for n in range(8):
                        c = first_col + UNIT_C * (2 * i + n // 4)
                        unit(base + n, view[n % 4][:, :, ds(c, UNIT_C)], i)
                if base == 0:
                    body(0)
                    base, first_col, blocks = base + 8, first_col + 2 * UNIT_C, blocks - 2
                if blocks == 2:
                    body(0)
                else:
                    with sp.Fori(0, blocks // 2) as i:
                        body(i)

            def k_view(m):
                return m.rearrange("(q k p) c -> q p k c", p=P, k=UNIT_K)

            def experts(layer, base):
                wg, wu = (w[n][layer].rearrange("e (q k p) f -> e q p k f", p=P, k=UNIT_K)
                          for n in ("moe_w_gate", "moe_w_up"))
                wd = w["moe_w_down"][layer].rearrange("e (k p) c -> e p k c", p=P)

                def sources(i):
                    for q in range(4):
                        for m in (wg, wu):
                            for e in range(2):
                                yield m[2 * i + e, q]
                    for d in range(4):
                        for e in range(2):
                            yield wd[2 * i + e][:, :, d * UNIT_C:(d + 1) * UNIT_C]

                for n, src in enumerate(sources(0)):
                    if n in EARLY:
                        k = n - EARLY[0]
                        sp.wait_ge(used, base)
                        sp.dma_start(EARLY_AT[k][:, :, :], src).then_inc(sem(f"early_loaded_{k // 4}"), 16)
                    else:
                        unit(base + n - (len(EARLY) if n > EARLY[-1] else 0), src)
                with sp.Fori(0, PAIRS - 1) as i:
                    for n, src in enumerate(sources(i + 1)):
                        unit(base - len(EARLY) + PAIR_UNITS + n, src, i, PAIR_UNITS)

            sp.wait_ge(sem("x_ready"), 16)
            sp.wait_ge(sem("consts_loaded"), 16)
            a_in = k_view(w["a_w_in"][0])
            matrix(U_QK, a_in, 4, 0)
            matrix(U_V, a_in, 4, QK_CH)
            matrix(U_O, a_in, 4, QK_CH + D)
            matrix(U_AOUT, k_view(w["a_w_out"][0]), 4, 0)
            experts(0, U_MOE0)
            b_in = k_view(w["b_w_in"][0])
            for n in range(4):
                unit(U_CKV + n, b_in[n][:, :, Q_COLS:Q_COLS + RANK])
            ukv = w["b_w_ukv"][0].rearrange("(k p) c -> p k c", p=P)
            for i in range(HEADS_B // 2):
                for n in range(4):
                    unit(U_PAIRS + 5 * i + n, b_in[n][:, :, i * PAIR_Q:(i + 1) * PAIR_Q])
                unit(U_PAIRS + 5 * i + 4, ukv[:, :, i * UNIT_C:(i + 1) * UNIT_C])
            matrix(U_BOUT, k_view(w["b_w_out"][0]), 4, 0)
            experts(1, U_MOE1)
            sp.wait_ge(sem("x_ready"), 16 + 2)
            sp.dma_start(out.rearrange("b (t p) d -> p (b t) d", p=P), X[:, :, :]).then_inc(sem("stored"), 16)
            sp.wait_ge(sem("stored"), 16)

        @block.gpsimd
        def _(pool):
            def low_parts(tag, tmp):
                for n in range(8):
                    g, t = divmod(n, NT)
                    pool.wait_ge(sem("xt_hi"), 8 * TURNS.index(tag) + n + 1)
                    o = (slice(None), slice(4 * g, 4 * g + 4), slice(t * P, (t + 1) * P))
                    pool.tensor_tensor(XTL[o], tmp[:, n % 2, :].rearrange("p (a b) -> p a b", a=4), XTH[o],
                                       ALU.subtract).then_inc(sem("xt_ready"), 1)

            low_parts("n0", a_["T"])
            low_parts("h", a_["T"])
            for l in range(2):
                if l:
                    low_parts("n2", b_["T"])
                    for g in range(4):
                        pool.wait_ge(sem("ot_hi"), g + 1)
                        pool.tensor_tensor(XTL[:, 4 * g:4 * g + 4, :], b_["OT"][:, 4 * g:4 * g + 4, :],
                                           XTH[:, 4 * g:4 * g + 4, :], ALU.subtract).then_inc(sem("ot_ready"), 1)
                pool.wait_ge(sem("routed"), l + 1)
                flag = pool.value_load(FLAG[0:1, l:l + 1], min_val=0, max_val=1)
                wg, wu = (w[n][l].rearrange("e (q k p) f -> e q p k f", p=P, k=UNIT_K)
                          for n in ("moe_w_gate", "moe_w_up"))
                wd = w["moe_w_down"][l].rearrange("e (k p) c -> e p k c", p=P)
                with pool.If(flag > 0):
                    with pool.Fori(0, EXTRA) as q:
                        with pool.Fori(0, PAIRS) as i:
                            j = q * PAIRS + i
                            srcs = [m[2 * i + e, k] for k in range(4) for m in (wg, wu) for e in range(2)]
                            srcs += [wd[2 * i + e][:, :, d * UNIT_C:(d + 1) * UNIT_C] for d in range(4) for e in range(2)]
                            for n, src in enumerate(srcs):
                                pool.wait_ge(sem(f"over_free_{l}"), j * PAIR_UNITS + n + 1)
                                pool.sem_inc(sem("over_turns"), 1)
                                pool.dma_start(OV[n % 4][:, :, :], src).then_inc(sem(f"over_loaded_{l}_{n % 4}"), 16)

        @block.tensor
        def _(pe):
            used = sem("unit_used")

            def transposes(tag):
                for n in range(8):
                    g, t = divmod(n, NT)
                    if g == 0:
                        pe.wait_ge(sem("xn_ready"), NT * TURNS.index(tag) + t + 1)
                    for k in range(4):
                        c = 4 * g + k
                        last = pe.transpose(PS[:, n, k * P:(k + 1) * P], XN[:, t, c * P:(c + 1) * P], IDENT)
                    last.then_inc(sem("turned"), 1)

            def three(out, l, r, first, last):
                pe.matmul(out, l[0], r[0], start=first, stop=False)
                pe.matmul(out, l[0], r[1], start=False, stop=False)
                return pe.matmul(out, l[1], r[0], start=False, stop=last)

            def token_unit(s, banks, lhs, k0, first, last, i=0):
                pe.wait_ge(sem("lo_ready"), s + 1 + 8 * i)
                n = width(s)
                for kk in range(UNIT_K):
                    for t in range(NT):
                        col = (slice(None), k0 + kk, slice(t * P, (t + 1) * P))
                        part = (HI[s % 2][:, kk, 0:n], LO[stream(s) % RING][:, kk, 0:n])
                        mm = three(PS[:, banks[t], 0:n], (lhs[0][col], lhs[1][col]), part,
                                   first and kk == 0, last and kk == UNIT_K - 1)
                mm.then_inc(used, 1)

            XTP = (XTH, XTL)

            def out_projection(l, first, free, tokens_ready, done):
                def turn(b):
                    for t in range(NT):
                        pe.wait_ge(sem(free), 4 + 2 * b + t + 1)
                        for k in range(4):
                            c = 4 * b + k
                            last = pe.transpose(PS[:, 4 + t, k * P:(k + 1) * P], X[:, t, c * P:(c + 1) * P], IDENT)
                        last.then_inc(sem("x_turned"), 1)

                def logits(b):
                    for t in range(NT):
                        pe.wait_ge(sem("x_columns"), 8 * l + 2 * b + t + 1)
                        for c in range(4 * b, 4 * b + 4):
                            last = pe.matmul(PS[:, 6 + t, 0:N_EXP], m_["XT"][:, c, t * P:(t + 1) * P], RW[:, c, :],
                                             start=(c == 0), stop=(c == DC - 1))
                    return last

                pe.wait_ge(sem("router_loaded"), 32)
                for b in range(4):
                    pe.wait_ge(sem(free), 2 * b + 2)
                    for n in range(done if b == 0 else 0, 4):
                        tokens_ready(n)
                        token_unit(first + 4 * b + n, OUT_BANKS[l][b], XTP, UNIT_K * n, n == 0, n == 3)
                        if b and n == 1:
                            turn(b - 1)
                        if b and n == 2:
                            logits(b - 1)
                turn(3)
                logits(3).then_inc(sem("logits"), 1)

            def chunks_ready(tag, n):
                pe.wait_ge(sem("xt_ready"), 8 * TURNS.index(tag) + NT * (n + 1))

            def few_columns(out, w_, n, t, tag):
                for k in range(DC):
                    if k % 4 == 0:
                        pe.wait_ge(sem("xt_ready"), 8 * TURNS.index(tag) + NT * (k // 4) + t + 1)
                    col = (slice(None), k, slice(t * P, (t + 1) * P))
                    mm = three(out, (XTH[col], XTL[col]), [v[:, k, 0:n] for v in w_], k == 0, k == DC - 1)
                return mm

            pe.wait_ge(sem("vectors_loaded"), 16 * 6)
            pe.wait_ge(sem("consts_loaded"), 16)
            pe.transpose(PS[:, 7, 0:V_ROWS], ROWS[0:V_ROWS, :], IDENT[0:V_ROWS, 0:V_ROWS])
            pe.transpose(PS[:, 7, 128:144], ROWS2[:, :], IDENT[0:16, 0:16]).then_inc(sem("vectors_turned"), 1)
            pe.wait_ge(sem("vec_ready"), 2)
            transposes("n0")
            pe.wait_ge(sem("few_lo"), 1)
            for t in range(NT):
                last = few_columns(PS[:, 0, t * N_GATES:(t + 1) * N_GATES], WGP, N_GATES, t, "n0")
            last.then_inc(sem("gates_done"), 1)
            pe.wait_ge(sem("gates_read"), 2)
            with pe.Fori(0, 2) as i:
                for b in range(2):
                    for n in range(4):
                        u = U_QK + 4 * b + n
                        pe.wait_ge(sem("lo_ready"), u + 1 + 8 * i)
                        for ch in range(4):
                            if n == 0:
                                pe.wait_ge(sem("qk_free"), 8 * i + 4 * b + ch + 1)
                            for kk in range(UNIT_K):
                                k = UNIT_K * n + kk
                                part = [v[:, kk, ch * P:(ch + 1) * P] for v in (HI[u % 2], LO[u % RING])]
                                last = three(PS[:, 4 * b + ch, 0:SEQ], part, (XTH[:, k, :], XTL[:, k, :]),
                                             k == 0, k == DC - 1)
                        last.then_inc(used, 1)

            def v_block(b):
                pe.wait_ge(sem("v_free"), 2 * b + 2)
                for n in range(4):
                    token_unit(U_V + 4 * b + n, (2 * (b % 2), 2 * (b % 2) + 1), XTP, UNIT_K * n, n == 0, n == 3)

            v_block(0)
            pe.wait_ge(sem("qk_free"), 8 + 16)
            for n in range(4):
                ty, t = divmod(n, 2)
                last = pe.transpose(PS[0:ROW, 6, n * P:(n + 1) * P], a_["GP"][:, 2 * ty + t, :], IDENT)
            last.then_inc(sem("gate_rows"), 1)
            v_block(1)
            v_block(2)
            pe.wait_ge(sem("scans_done"), 1)
            pe.wait_ge(sem("rows_ready_act"), 3)
            for n in range(8):
                c, q = divmod(n, 4)
                last = pe.transpose(PS[:, 7, n * ROW:(n + 1) * ROW], a_["RQ"][0:ROW, q, c * P:(c + 1) * P],
                                    IDENT[0:ROW, 0:ROW])
            last.then_inc(sem("cols_turned"), 1)
            v_block(3)

            VA, QKT = a_["VA"], a_["QKT"]
            for h in range(HEADS_A):
                def o_unit(n):
                    u = U_O + 2 * h + n
                    if n == 0 and h % 2 == 0:
                        pe.wait_ge(sem("o_free"), h + 2)
                    q = (2 * h + n) % 4
                    token_unit(u, (6, 7), XTP, UNIT_K * q, q == 0, q == 3)

                q_t = [QKT[:, h, c * P:(c + 1) * P] for c in range(2)]
                k_t = [QKT[:, 8 + h, c * P:(c + 1) * P] for c in range(2)]
                pe.wait_ge(sem("r_staged"), h + 1)
                pe.matmul(PS[:, 1, :], ONES[0:ROW, :], a_["RSEL"][0:ROW, h % 2, :], start=True, stop=True)\
                    .then_inc(sem("r_spread"), 1)
                if h:
                    pe.wait_ge(sem("intra_ready"), 4 * h)
                else:
                    pe.wait_ge(sem("v_free"), 4 + 2 * (D // UNIT_C))
                for c in range(2):
                    last = pe.transpose(PS[:, 2, c * P:(c + 1) * P], k_t[c], IDENT)
                last.then_inc(sem("k_turned"), 1)
                for c in range(2):
                    last = pe.matmul(PS[:, 0, c * P:(c + 1) * P], k_t[c], q_t[c], start=True, stop=True)
                last.then_inc(sem("scores_a"), 1)
                o_unit(0)
                if h:
                    pe.wait_ge(sem("inter_read"), h)
                pe.wait_ge(sem("kw_ready"), h + 1)
                for d in range(2):
                    last = pe.matmul(PS[:, 3 + d, 0:DV_A + 1], a_["KW"][:, d, :], VA[:, d, h, 0:DV_A + 1],
                                     start=True, stop=True)
                last.then_inc(sem("state_done"), 1)
                o_unit(1)
                pe.wait_ge(sem("state_ready"), h + 1)
                for d in range(2):
                    last = pe.matmul(PS[:, 3 + d, 0:DV_A + 1], q_t[1 - d], a_["CS"][:, d, 0:DV_A + 1],
                                     start=True, stop=True)
                last.then_inc(sem("inter_done"), 1)
                pe.wait_ge(sem("dt_ready"), h + 1)
                for j in range(4):
                    d, c = divmod(j, 2)
                    if j >= 2:
                        pe.wait_ge(sem("intra_ready"), 4 * h + j - 1)
                    pe.matmul(PS[:, (5, 2)[j % 2], 0:DV_A + 1], a_["DT"][:, d, c * P:(c + 1) * P],
                              VA[:, c, h, 0:DV_A + 1], start=True, stop=True).then_inc(sem("intra_done"), 1)
            transposes("h")
            out_projection(0, U_AOUT, "aout_free", lambda n: chunks_ready("h", n), 0)

            def route(l):
                pe.wait_ge(sem("mask_ready"), l + 1)
                MK = m_["MK"]
                pe.matmul(PS[:, 1, 0:N_EXP], TRI, MK[:, 0, :], start=True, stop=True)
                pe.matmul(PS[:, 1, N_EXP:2 * N_EXP], ONES, MK[:, 0, :], start=True, stop=False)
                pe.matmul(PS[:, 1, N_EXP:2 * N_EXP], TRI, MK[:, 1, :], start=False, stop=True)
                pe.matmul(PS[:, 1, 2 * N_EXP:3 * N_EXP], ONES, MK[:, 0, :], start=True, stop=False)
                pe.matmul(PS[:, 1, 2 * N_EXP:3 * N_EXP], ONES, MK[:, 1, :], start=False, stop=True)\
                    .then_inc(sem("positions"), 1)

            def experts(l, base):
                def gather(m, j):
                    pe.wait_ge(sem(m + "sel_ready"), j + 1)
                    for g in range(4):
                        bank = 2 + g % 2
                        if g >= 2:
                            pe.wait_ge(sem(m + "xg_ready"), 4 * j + g - 1)
                        for k in range(4):
                            c = 4 * g + k
                            for t in range(NT):
                                last = pe.matmul(PS[:, bank, k * P:(k + 1) * P], XN[:, t, c * P:(c + 1) * P],
                                                 m_["SEL"][:, t, :], start=(t == 0), stop=(t == NT - 1))
                        last.then_inc(sem(m + "gathered"), 1)

                def pair(m, j, arrived, slot, consumed, following, uncounted=()):
                    pe.wait_ge(sem(m + "xg_ready"), 4 * j + 4)
                    for q in range(4):
                        for n in range(4):
                            arrived(4 * q + n)
                        for kk in range(UNIT_K):
                            k = UNIT_K * q + kk
                            for up in range(2):
                                for e in range(2):
                                    n = 4 * q + 2 * up + e
                                    last = pe.matmul(PS[64 * e:64 * e + 64, up, :], m_["XG"][:, k, 64 * e:64 * e + 64],
                                                     slot(n)[:, kk, :], start=(k == 0), stop=(k == DC - 1))
                                    if kk == UNIT_K - 1 and n not in uncounted:
                                        last.then_inc(consumed, 1)
                    if following:
                        gather(m, j + 1)
                    pe.wait_ge(sem(m + "a_ready"), j + 1)
                    for c in range(FC):
                        last = pe.transpose(PS[:, 4, c * P:(c + 1) * P], m_["A"][:, c * P:(c + 1) * P], IDENT)
                    last.then_inc(sem(m + "a_turned"), 1)
                    for t in range(NT):
                        last = pe.transpose(PS[:, 5, t * P:(t + 1) * P], m_["SELG"][:, t, :], IDENT)
                    last.then_inc(sem(m + "sel_turned"), 1)
                    pe.wait_ge(sem(m + "at_ready"), j + 1)

                    def scatter(d):
                        pe.wait_ge(sem(m + "y_ready"), 4 * j + d + 1)
                        for t in range(NT):
                            if d > 0:
                                pe.wait_ge(sem(m + "x_added"), 8 * j + 2 * d + t - 1)
                            pe.matmul(PS[:, 2 + t, :], m_["SCT"][:, t * P:(t + 1) * P], m_["YS"][:, d, :],
                                      start=True, stop=True).then_inc(sem(m + "scattered"), 1)

                    for d in range(4):
                        for e in range(2):
                            arrived(16 + 2 * d + e)
                        for c in range(FC):
                            for e in range(2):
                                last = pe.matmul(PS[64 * e:64 * e + 64, 6 + d % 2, :], m_["AT"][:, c, 64 * e:64 * e + 64],
                                                 slot(16 + 2 * d + e)[:, c, :], start=(c == 0), stop=(c == FC - 1))
                                if c == FC - 1:
                                    last.then_inc(consumed, 1)
                        if d == 0:
                            if following:
                                pe.wait_ge(sem(m + "xg_ready"), 4 * j + 8)
                            pe.wait_ge(sem(m + "sct_ready"), j + 1)
                        else:
                            scatter(d - 1)
                    scatter(3)

                m = "m_"
                pe.wait_ge(sem("xn_ffn"), NT * (l + 1))
                gather(m, PAIRS * l)

                def place(n):
                    return base + n - (len(EARLY) if n > EARLY[-1] else 0)

                def first_arrived(n):
                    if n in EARLY:
                        k = (n - EARLY[0]) // 4
                        pe.wait_ge(sem(f"early_loaded_{k}"), 16 * (4, 2)[k] * (l + 1))
                    else:
                        unit_arrived(pe, place(n))

                pair(m, PAIRS * l, first_arrived,
                     lambda n: EARLY_AT[n - EARLY[0]] if n in EARLY else ring[place(n) % RING], used, True, EARLY)
                later = base - len(EARLY) + PAIR_UNITS

                def main(i, following):
                    pair(m, i + 1 + PAIRS * l, lambda n: unit_arrived(pe, later + n, i, PAIR_UNITS),
                         lambda n: ring[(later + n) % RING], used, following)
                with pe.Fori(0, PAIRS - 2) as i:
                    main(i, True)
                main(PAIRS - 2, False)
                m = f"o{l}_"
                flag = pe.value_load(FLAG[0:1, l:l + 1], min_val=0, max_val=1)
                with pe.If(flag > 0):
                    with pe.Fori(0, EXTRA) as q:
                        with pe.Fori(0, PAIRS) as i:
                            j = q * PAIRS + i
                            gather(m, j)
                            pair(m, j,
                                 lambda n: pe.wait_ge(sem(f"over_loaded_{l}_{n % 4}"),
                                                      16 * (PAIR_UNITS // 4) * j + 16 * (n // 4 + 1)),
                                 lambda n: OV[n % 4], sem(f"over_free_{l}"), False)

            route(0)
            experts(0, U_MOE0)

            transposes("n2")
            for n in range(4):
                chunks_ready("n2", n)
                token_unit(S_CKV + n, (0, 1), XTP, UNIT_K * n, n == 0, n == 3)
            pe.wait_ge(sem("few_lo"), 2)
            for t in range(NT):
                last = few_columns(PS[:, 4, t * ROPE:(t + 1) * ROPE], WKRP, ROPE, t, "n2")
            last.then_inc(sem("krope_done"), 1)

            def q_unit(i, n):
                if n == 0 and i:
                    pe.wait_ge(sem("q_read"), 2 * i)
                token_unit(S_PAIRS + 5 * i + n, (6, 7), XTP, UNIT_K * n, n == 0, n == 3)

            def kv_unit(i):
                token_unit(S_PAIRS + 5 * i + 4, (4, 5), (CKH, CKL), 0, True, True)

            def out_unit(n):
                pe.wait_ge(sem("ot_ready"), n + 1)
                token_unit(S_BOUT + n, OUT_BANKS[1][0], XTP, UNIT_K * n, n == 0, False)

            q_unit(0, 0)
            q_unit(0, 1)
            pe.wait_ge(sem("ckv_normed"), 2)
            for t in range(NT):
                for c in range(RC):
                    last = pe.transpose(PS[:, 2 + t, c * P:(c + 1) * P], b_["CKV"][:, t, c * P:(c + 1) * P], IDENT)
            last.then_inc(sem("ckv_turned"), 1)
            q_unit(0, 2)
            q_unit(0, 3)
            pe.wait_ge(sem("ckt_ready"), 2)
            pe.wait_ge(sem("krope_copied"), 1)
            kv_unit(0)
            for i in range(HEADS_B // 2):
                more = i + 1 < HEADS_B // 2
                V = [b_["KVP"][:, 2 * (i % 2) + s, :].rearrange("p (h c) -> p h c", h=2)[:, :, NOPE:] for s in range(NT)]
                if more:
                    q_unit(i + 1, 0)
                    q_unit(i + 1, 1)
                for p in range(2):
                    h = 2 * i + p
                    pe.wait_ge(sem("qk_normed"), h + 1)
                    if i:
                        pe.wait_ge(sem("o_copied"), h - 1)
                    for t in range(NT):
                        pe.transpose(PS[:, p, t * P:(t + 1) * P], QN[p][:, t, 0:NOPE], IDENT)
                        last = pe.transpose(PS[:, p, SEQ + t * P:SEQ + (t + 1) * P], KN[p][:, t, 0:NOPE], IDENT)
                    last.then_inc(sem("nope_turned"), 1)
                    for t in range(NT):
                        pe.transpose(PS[0:ROPE, 2 + p, t * P:(t + 1) * P], QN[p][:, t, NOPE:DQ_B], IDENT)
                        last = pe.transpose(PS[0:ROPE, 2 + p, SEQ + t * P:SEQ + (t + 1) * P],
                                            KN[p][:, t, NOPE:DQ_B], IDENT)
                    last.then_inc(sem("rope_turned"), 1)
                if more:
                    q_unit(i + 1, 2)
                else:
                    pe.wait_ge(sem("q_read"), HEADS_B)
                    out_unit(0)
                pe.wait_ge(sem("kv_read"), 2 * i + 2)
                for p in range(2):
                    h = 2 * i + p
                    pe.wait_ge(sem("nope_ready"), h + 1)
                    pe.wait_ge(sem("rope_ready"), h + 1)
                    for t in range(NT):
                        o = PS[:, 4 + p, t * SEQ:(t + 1) * SEQ]
                        pe.matmul(o, QKN[p][:, t * P:(t + 1) * P], QKN[p][:, SEQ:2 * SEQ], start=True, stop=False)
                        last = pe.matmul(o, QKR[p][0:ROPE, t * P:(t + 1) * P], QKR[p][0:ROPE, SEQ:2 * SEQ],
                                         start=False, stop=True)
                    last.then_inc(sem("scores_b"), 1)
                if more:
                    q_unit(i + 1, 3)
                else:
                    out_unit(1)
                for p in range(2):
                    h = 2 * i + p
                    pe.wait_ge(sem("probs_ready"), h + 1)
                    for t in range(NT):
                        for s in range(NT):
                            last = pe.transpose(PS[:, 2 + p, s * SEQ + t * P:s * SEQ + (t + 1) * P],
                                                PR[p][:, t, s * P:(s + 1) * P], IDENT)
                    last.then_inc(sem("probs_turned"), 1)
                if more:
                    kv_unit(i + 1)
                else:
                    out_unit(2)
                for p in range(2):
                    h = 2 * i + p
                    pe.wait_ge(sem("pt_ready"), h + 1)
                    for s in range(NT):
                        last = pe.matmul(PS[:, p, 0:SEQ], V[s][:, p, :], PT[p][:, s, :], start=(s == 0), stop=(s == NT - 1))
                    last.then_inc(sem("o_done"), 1)
            out_projection(1, S_BOUT, "bout_free", lambda n: pe.wait_ge(sem("ot_ready"), n + 1), 3)
            route(1)
            experts(1, U_MOE1)

        @block.scalar
        def _(act):
            load = act.dma_start
            load(X[:, :, :], w["x"].rearrange("b (t p) d -> p (b t) d", p=P)).then_inc(sem("x_ready"), 16)
            load(CON[:, :], w["consts"]).then_inc(sem("consts_loaded"), 16)
            load(ROWS[V_MIX:V_MIX + 32, :], w["norm_mix"].rearrange("l (c p) -> (l c) p", p=P)).then_inc(sem("vectors_loaded"), 16)
            load(ROWS[V_FFN:V_FFN + 32, :], w["norm_ffn"].rearrange("l (c p) -> (l c) p", p=P)).then_inc(sem("vectors_loaded"), 16)
            load(ROWS[V_CONV:V_CONV + 48, :], w["a_conv_w"].rearrange("a k (c p) -> (a k c) p", p=P)).then_inc(sem("vectors_loaded"), 16)
            load(ROWS[V_KV:V_KV + 4, :], w["b_kv_norm"].rearrange("a (c p) -> (a c) p", p=P)).then_inc(sem("vectors_loaded"), 16)
            load(ROWS2, w["a_out_norm"].rearrange("a (c p) -> (a c) p", p=P)).then_inc(sem("vectors_loaded"), 16)
            load(a_["GB"], w["a_gate_b"].broadcast_to([P, N_GATES])).then_inc(sem("vectors_loaded"), 16)
            load(a_["WG"], w["a_w_in"][0].rearrange("(c p) n -> p c n", p=P)[:, :, QK_CH + 2 * D:]).then_inc(sem("wg_loaded"), 16)
            load(RW[:, :, :], w["router_w"].rearrange("(c p) n -> p c n", p=P)).then_inc(sem("router_loaded"), 16)
            load(RB[:, :], w["router_b"].rearrange("(a n) -> a n", a=1).broadcast_to([P, N_EXP])).then_inc(sem("router_loaded"), 16)

            def high(s):
                u, n = stream(s), width(s)
                unit_arrived(act, u)
                if s >= 2:
                    act.wait_ge(sem("unit_used"), stream(s - 2) + 1)
                act.activation(HI[s % 2][:, :, 0:n], ring[u % RING][:, :, 0:n], ACT.Copy).then_inc(sem("hi_ready"), 1)

            def high_tokens(tag, tmp):
                for n in range(8):
                    g, t = divmod(n, NT)
                    act.wait_ge(sem("xt_tmp"), 8 * TURNS.index(tag) + n + 1)
                    act.activation(XTH[:, 4 * g:4 * g + 4, t * P:(t + 1) * P],
                                   tmp[:, n % 2, :].rearrange("p (a b) -> p a b", a=4), ACT.Copy).then_inc(sem("xt_hi"), 1)

            def norm(tag):
                at = NORMS.index(tag)
                act.wait_ge(sem("x_ready"), 16 + at)
                for t in range(NT):
                    if t:
                        act.wait_ge(sem("squares"), NT * at + t)
                    act.activation(XN[:, t, :], X[:, t, :], ACT.Square, accum_out=SSQ[:, t:t + 1]).then_inc(sem("squares"), 1)
                act.wait_ge(sem("means"), 2 * at + 1)
                act.activation(SSQ[:, 4:6], SSQ[:, 2:4], ACT.Sqrt).then_inc(sem("roots"), 1)

            norm("n0")
            act.wait_ge(sem("wg_loaded"), 16)
            act.activation(WGP[0][:, :, :], a_["WG"], ACT.Copy).then_inc(sem("few_hi"), 1)
            high_tokens("n0", a_["T"])
            high(0)
            high(1)
            act.wait_ge(sem("pads_zeroed"), 1)
            act.drain().then_inc(sem("qk_free"), 8)

            def pad(c):
                act.wait_ge(sem("unit_used"), U_QK + 4 * (c // 4) + 4)
                if c >= 2:
                    act.wait_ge(sem("conv_done"), c - 1)
                act.activation(a_["PAD"][:, c % 2, 1:SEQ + 1], PS[:, c % 8, 0:SEQ], ACT.Copy).then_inc(sem("qk_free"), 1)

            def sigmoid(c):
                act.wait_ge(sem("conv_done"), c + 1)
                act.activation(a_["SGC"][:, c % 2, :], a_["CT"][:, c % 2, :], ACT.Sigmoid).then_inc(sem("conv_sig"), 1)

            for u in range(2, U_V + 4):
                high(u)
                if u >= 4:
                    pad(u - 4)
                if u >= 5:
                    sigmoid(u - 5)
                if u == U_V - 1:
                    act.drain().then_inc(sem("v_free"), 4)
            high(U_V + 4)
            sigmoid(15)

            def v_copy(b):
                act.wait_ge(sem("unit_used"), U_V + 4 * b + 4)
                for t in range(NT):
                    act.activation(a_["VA"][:, t, 2 * b:2 * b + 2, 0:DV_A],
                                   PS[:, 2 * (b % 2) + t, :].rearrange("p (a b) -> p a b", a=2), ACT.Copy)\
                        .then_inc(sem("v_free"), 1)

            high(U_V + 5)
            v_copy(0)
            act.wait_ge(sem("abs_ready"), 1)
            act.activation(a_["T1"][0:ROW, :], a_["T1"][0:ROW, :], ACT.Exp, scale=-1.0).then_inc(sem("gate_functions"), 1)
            act.wait_ge(sem("gate_functions"), 1)
            act.activation(a_["T1"][0:ROW, :], a_["T1"][0:ROW, :], ACT.Ln, bias=1.0).then_inc(sem("gate_functions"), 1)
            high(U_V + 6)
            act.wait_ge(sem("scans_done"), 1)
            RQ, R, MP = a_["RQ"], a_["R"], a_["MP"]
            for d in range(2):
                rows = slice(0, 32) if d == 0 else slice(32, ROW)
                c1, c2 = (0, 1) if d == 0 else (1, 0)
                act.activation(RQ[rows, 1, c2 * P:(c2 + 1) * P], R[rows, c2 * P:(c2 + 1) * P], ACT.Exp,
                               bias=MP[rows, 0:1], scale=-1.0)
                last = act.activation(RQ[rows, 3, c1 * P:(c1 + 1) * P], RQ[rows, 0, c1 * P:(c1 + 1) * P], ACT.Exp,
                                      bias=MP[rows, 1:2])
                last.then_inc(sem("rows_ready_act"), 1)
            act.activation(RQ[0:ROW, 2, :], a_["T2"][0:ROW, :], ACT.Exp, scale=-1.0).then_inc(sem("rows_ready_act"), 1)

            for u in range(U_V + 7, U_O + 1):
                high(u)
                if u % 4 == 1:
                    v_copy((u - U_V) // 4 - 1)
            v_copy(3)
            act.drain().then_inc(sem("o_free"), 2)
            for h in range(HEADS_A):
                u = U_O + 2 * h
                act.wait_ge(sem("k_turned"), h + 1)
                for d in range(2):
                    last = act.activation(a_["KW"][:, d, :], PS[:, 2, d * P:(d + 1) * P], ACT.Copy,
                                          scale=a_["COLT"][:, 4 * d + 3, h + 32 * d:h + 32 * d + 1])
                last.then_inc(sem("kw_ready"), 1)
                high(u + 1)
                act.wait_ge(sem("z_ready"), h + 1)
                act.activation(a_["Z"], a_["Z"], ACT.Exp, scale=-1.0).then_inc(sem("decay_ready"), 1)
                act.wait_ge(sem("state_done"), h + 1)
                for d in range(2):
                    last = act.activation(a_["CS"][:, d, 0:DV_A + 1], PS[:, 3 + d, 0:DV_A + 1], ACT.Copy)
                last.then_inc(sem("state_ready"), 1)
                high(u + 2)
                if h % 2:
                    act.wait_ge(sem("unit_used"), u + 2)
                    if h >= 3:
                        act.wait_ge(sem("gated"), h - 1)
                    for t in range(NT):
                        act.activation(a_["OGS"][:, t, :], PS[:, 6 + t, :], ACT.Sigmoid).then_inc(sem("o_free"), 1)
                for j in range(4):
                    act.wait_ge(sem("intra_done"), 4 * h + j + 1)
                    act.activation(a_["NS"][:, j, 0:DV_A + 1], PS[:, (5, 2)[j % 2], 0:DV_A + 1], ACT.Copy)\
                        .then_inc(sem("intra_ready"), 1)
            act.wait_ge(sem("head_sums"), 1)
            act.activation(SMA[:, 1, :], SMA[:, 0, :], ACT.Sqrt).then_inc(sem("head_roots"), 1)
            high(U_AOUT + 1)
            high_tokens("h", a_["T"])

            def residual(l, first, free, start):
                def squares(b):
                    for t in range(NT):
                        act.wait_ge(sem(free), 4 + 2 * b + t + 1)
                        xs = (slice(None), t, slice(UNIT_C * b, UNIT_C * (b + 1)))
                        act.activation(XN[xs], X[xs], ACT.Square, accum_out=SSB[:, t, b:b + 1])\
                            .then_inc(sem("square_parts"), 1)

                for n in range(start, 16):
                    high(first + n)
                    if n % 4 == 3 and n > 3:
                        squares(n // 4 - 1)
                squares(3)
                act.wait_ge(sem("means"), 2 * l + 2)
                act.activation(SSQ[:, 4:6], SSQ[:, 2:4], ACT.Sqrt).then_inc(sem("roots"), 1)

            residual(0, U_AOUT, "aout_free", 2)

            def experts(l, base):
                act.wait_ge(sem("logits"), l + 1)
                act.wait_ge(sem("ffn_norm"), l + 1)
                for t in range(NT):
                    act.activation(m_["SC"][:, t, :], PS[:, 6 + t, 0:N_EXP], ACT.Sigmoid, scale=SSQ[:, 6 + t:7 + t])\
                        .then_inc(sem("scores"), 1)
                for t in range(NT):
                    act.activation(XN[:, t, :], X[:, t, :], ACT.Copy, scale=SSQ[:, 6 + t:7 + t]).then_inc(sem("xn_ffn"), 1)

                def pair(m, j, products):
                    products(16)
                    act.activation(m_["SIG"], PS[:, 0, :], ACT.Sigmoid).then_inc(sem(m + "sig"), 1)
                    act.wait_ge(sem(m + "a_turned"), j + 1)
                    act.activation(m_["AT"], ps4(4), ACT.Copy).then_inc(sem(m + "at_ready"), 1)
                    for d in range(4):
                        products(16 + 2 * (d + 1))
                        act.activation(m_["YS"][:, d, :], PS[:, 6 + d % 2, :], ACT.Copy).then_inc(sem(m + "y_ready"), 1)

                with act.Fori(0, PAIRS) as i:
                    pair("m_", i + PAIRS * l, lambda n: act.wait_ge(sem("unit_used"), base - len(EARLY) + PAIR_UNITS * i + n))
                flag = act.value_load(FLAG[0:1, l:l + 1], min_val=0, max_val=1)
                with act.If(flag > 0):
                    with act.Fori(0, EXTRA) as q:
                        with act.Fori(0, PAIRS) as i:
                            j = q * PAIRS + i
                            pair(f"o{l}_", j, lambda n: act.wait_ge(sem(f"over_free_{l}"), 4 + PAIR_UNITS * j + n))

            experts(0, U_MOE0)

            high(S_CKV)
            high(S_CKV + 1)
            norm("n2")
            load(b_["WKR"], w["b_w_in"][0].rearrange("(c p) n -> p c n", p=P)[:, :, Q_COLS + RANK:]).then_inc(sem("wkr_loaded"), 16)
            load(b_["QG"], w["b_q_norm"].broadcast_to([P, DQ_B])).then_inc(sem("qk_gains"), 16)
            load(b_["KG"], w["b_k_norm"].broadcast_to([P, DQ_B])).then_inc(sem("qk_gains"), 16)
            high_tokens("n2", b_["T"])
            act.wait_ge(sem("wkr_loaded"), 16)
            act.activation(WKRP[0][:, :, :], b_["WKR"], ACT.Copy).then_inc(sem("few_hi"), 1)
            high(S_CKV + 2)
            high(S_CKV + 3)
            high(S_PAIRS)
            act.wait_ge(sem("unit_used"), U_CKV + 4)
            for t in range(NT):
                act.activation(b_["CKV"][:, t, :], PS[:, t, :], ACT.Copy).then_inc(sem("ckv_copied"), 1)
            high(S_PAIRS + 1)
            act.wait_ge(sem("krope_done"), 1)
            act.activation(b_["KR"], PS[:, 4, 0:NT * ROPE].rearrange("p (t r) -> p t r", t=NT), ACT.Copy)\
                .then_inc(sem("krope_copied"), 1)
            act.wait_ge(sem("ckv_means"), 1)
            act.activation(SSQ[:, 4:6], SSQ[:, 2:4], ACT.Sqrt).then_inc(sem("ckv_roots"), 1)
            high(S_PAIRS + 2)
            for t in range(NT):
                act.wait_ge(sem("ckt_tmp"), t + 1)
                act.activation(CKH[:, :, t * P:(t + 1) * P], b_["T"][:, t, :].rearrange("p (a b) -> p a b", a=4), ACT.Copy)\
                    .then_inc(sem("ckt_hi"), 1)

            def q_copy(i):
                act.wait_ge(sem("unit_used"), U_PAIRS + 5 * i + 4)
                if i:
                    act.wait_ge(sem("qk_normed"), 2 * i)
                for t in range(NT):
                    act.activation(b_["QP"][:, t, :], PS[:, 6 + t, 0:PAIR_Q], ACT.Copy).then_inc(sem("q_read"), 1)

            def out_high(g):
                act.activation(XTH[:, 4 * g:4 * g + 4, :], b_["OT"][:, 4 * g:4 * g + 4, :], ACT.Copy).then_inc(sem("ot_hi"), 1)

            high(S_PAIRS + 3)
            high(S_PAIRS + 4)
            q_copy(0)
            high(S_PAIRS + 5)
            for i in range(HEADS_B // 2):
                more = i + 1 < HEADS_B // 2
                s = S_PAIRS + 5 * (i + 1)
                high(s + 1)
                act.wait_ge(sem("unit_used"), U_PAIRS + 5 * i + 5)
                for t in range(NT):
                    act.activation(b_["KVP"][:, 2 * (i % 2) + t, :], PS[:, 4 + t, :], ACT.Copy).then_inc(sem("kv_read"), 1)
                act.wait_ge(sem("qk_means"), i + 1)
                act.activation(b_["RT"], b_["SS"], ACT.Sqrt).then_inc(sem("qk_roots"), 1)
                if not more:
                    act.wait_ge(sem("unit_used"), U_PAIRS + 5 * i + 4)
                    act.wait_ge(sem("o_copied"), 12)
                    for g in range(3):
                        out_high(g)
                if more:
                    high(s + 2)
                for p in range(2):
                    h = 2 * i + p
                    act.wait_ge(sem("nope_turned"), h + 1)
                    act.activation(QKN[p], PS[:, p, :], ACT.Copy).then_inc(sem("nope_ready"), 1)
                    act.wait_ge(sem("rope_turned"), h + 1)
                    act.activation(QKR[p][0:ROPE, :], PS[0:ROPE, 2 + p, :], ACT.Copy).then_inc(sem("rope_ready"), 1)
                if more:
                    high(s + 3)
                for p in range(2):
                    h = 2 * i + p
                    act.wait_ge(sem("max_ready"), h + 1)
                    for t in range(NT):
                        act.activation(PR[p][:, t, :], PS[:, 4 + p, t * SEQ:(t + 1) * SEQ], ACT.Exp,
                                       bias=SM[:, p, t:t + 1], accum_out=SM[:, p, 2 + t:3 + t]).then_inc(sem("exp_done"), 1)
                if more:
                    high(s + 4)
                    q_copy(i + 1)
                else:
                    high(s + 2)
                for p in range(2):
                    h = 2 * i + p
                    act.wait_ge(sem("probs_turned"), h + 1)
                    act.activation(PT[p], PS[:, 2 + p, :].rearrange("p (a b) -> p a b", a=2), ACT.Copy)\
                        .then_inc(sem("pt_ready"), 1)
                high(s + 5 if more else s + 3)
                for p in range(2):
                    h = 2 * i + p
                    act.wait_ge(sem("o_done"), h + 1)
                    act.activation(b_["OT"][:, h, :], PS[:, p, 0:SEQ], ACT.Copy).then_inc(sem("o_copied"), 1)
            act.wait_ge(sem("o_copied"), HEADS_B)
            out_high(3)
            residual(1, S_BOUT, "bout_free", 4)
            experts(1, U_MOE1)

        @block.vector
        def _(dve):
            tt, ts, stt, red = dve.tensor_tensor, dve.tensor_scalar, dve.scalar_tensor_tensor, dve.tensor_reduce

            dve.wait_ge(sem("vectors_turned"), 1)
            dve.tensor_copy(VEC[:, 0:V_ROWS], PS[:, 7, 0:V_ROWS]).then_inc(sem("vec_ready"), 1)
            dve.tensor_copy(VEC[:, V_OUT:V_ALL], PS[:, 7, 128:144]).then_inc(sem("vec_ready"), 1)
            dve.wait_ge(sem("vec_ready"), 2)

            link = Chain(dve, sem("vector_chain"))

            def norm(tag):
                at = NORMS.index(tag)
                dve.wait_ge(sem("squares"), NT * (at + 1))
                ts(SSQ[:, 2:4], SSQ[:, 0:2], 1.0 / D, EPS, ALU.mult, ALU.add).then_inc(sem("means"), 1)
                dve.wait_ge(sem("roots"), 2 * at + 1)
                link(dve.reciprocal(SSQ[:, 6:8], SSQ[:, 4:6]))
                for t in range(NT):
                    ts(XN[:, t, :], X[:, t, :], SSQ[:, 6 + t:7 + t], None, ALU.mult).then_inc(sem("xn_ready"), 1)

            def low(s):
                u, n = stream(s), width(s)
                dve.wait_ge(sem("hi_ready"), s + 1)
                tt(LO[u % RING][:, :, 0:n], ring[u % RING][:, :, 0:n], HI[s % 2][:, :, 0:n], ALU.subtract)\
                    .then_inc(sem("lo_ready"), 1)

            def turned(tag, gain, tmp):
                for n in range(8):
                    g, t = divmod(n, NT)
                    dve.wait_ge(sem("turned"), 8 * TURNS.index(tag) + n + 1)
                    if n >= 2:
                        dve.wait_ge(sem("xt_ready"), 8 * TURNS.index(tag) + n - 1)
                    tt(tmp[:, n % 2, :].rearrange("p (a b) -> p a b", a=4), ps4(n), vec4(gain + 4 * g), ALU.mult)\
                        .then_inc(sem("xt_tmp"), 1)

            norm("n0")
            dve.wait_ge(sem("few_hi"), 1)
            tt(WGP[1][:, :, :], a_["WG"], WGP[0][:, :, :], ALU.subtract).then_inc(sem("few_lo"), 1)
            turned("n0", V_MIX, a_["T"])

            low(0)
            GP = a_["GP"]
            dve.wait_ge(sem("turned"), 8)
            link(dve.memset(GP, 0.0))
            dve.wait_ge(sem("gates_done"), 1)
            for d in range(2):
                for t in range(NT):
                    g0 = 16 * d
                    last = tt(GP[:, :, :].rearrange("p (y t) r -> p t y r", t=2)[:, t, :, 32 * d:32 * d + 8],
                              PS[:, 0, t * N_GATES + g0:t * N_GATES + g0 + 16].rearrange("p (y h) -> p y h", y=2),
                              a_["GB"][:, g0:g0 + 16].rearrange("p (y h) -> p y h", y=2), ALU.add)
                last.then_inc(sem("gates_read"), 1)
            dve.memset(a_["PAD"], 0.0).then_inc(sem("pads_zeroed"), 1)
            dve.memset(a_["VA"][:, :, :, DV_A:VW], 1.0)
            PAD, CT, SGC = a_["PAD"], a_["CT"], a_["SGC"]

            def conv(c):
                p = c % 2
                dve.wait_ge(sem("qk_free"), 8 + c + 1)
                if c >= 2:
                    dve.wait_ge(sem("qk_ready"), c - 1)
                link(ts(CT[:, p, :], PAD[:, p, 1:SEQ + 1], vec(V_CONV + 16 + c), None, ALU.mult))
                link(stt(CT[:, p, :], PAD[:, p, 0:SEQ], vec(V_CONV + c), CT[:, p, :], ALU.mult, ALU.add))
                stt(CT[:, p, :], PAD[:, p, 2:SEQ + 2], vec(V_CONV + 32 + c), CT[:, p, :], ALU.mult, ALU.add)\
                    .then_inc(sem("conv_done"), 1)

            def silu(c):
                dve.wait_ge(sem("conv_sig"), c + 1)
                stt(a_["QKT"][:, c, :], CT[:, c % 2, :], DQK_A ** -0.5 if c < HEADS_A else 1.0, SGC[:, c % 2, :],
                    ALU.mult, ALU.mult).then_inc(sem("qk_ready"), 1)

            for u in range(1, U_V + 4):
                low(u)
                if u >= 4:
                    conv(u - 4)
                if u >= 5:
                    silu(u - 5)
            low(U_V + 4)
            silu(15)
            low(U_V + 5)

            LI, LF, T1, T2, B, R, RQ, MP = (a_[n] for n in ("LI", "LF", "T1", "T2", "B", "R", "RQ", "MP"))
            dve.wait_ge(sem("gate_rows"), 1)
            dve.tensor_copy(LI[0:ROW, :], PS[0:ROW, 6, 0:SEQ])
            dve.memset(RQ[0:ROW, :, :], 0.0)
            link(dve.tensor_copy(LF[0:ROW, :], PS[0:ROW, 6, SEQ:2 * SEQ]))
            stt(T1[0:ROW, :], LF[0:ROW, :], -1.0, LF[0:ROW, :], ALU.mult, ALU.max).then_inc(sem("abs_ready"), 1)
            link(ts(LF[0:ROW, :], LF[0:ROW, :], 0.0, None, ALU.min))
            dve.wait_ge(sem("gate_functions"), 2)
            link(tt(LF[0:ROW, :], LF[0:ROW, :], T1[0:ROW, :], ALU.subtract))

            def span(v, d, c):
                rows = slice(0, 32) if d == 0 else slice(32, ROW)
                s = v[rows, c * P:(c + 1) * P]
                return s if d == 0 else s[:, ::-1]

            def one(v, d, at):
                rows = slice(0, 32) if d == 0 else slice(32, ROW)
                return v[rows, at:at + 1]

            for d in range(2):
                for c in range(2):
                    last = dve.tensor_tensor_scan(span(B, d, c), span(CON[:, C_ONE:C_ONE + SEQ], d, 0), span(LF, d, c), 0.0,
                                                  ALU.mult, ALU.add)
            link(last)
            link(tt(RQ[0:ROW, 0, :], LI[0:ROW, :], B[0:ROW, :], ALU.subtract))
            for d in range(2):
                c1 = d
                last = dve.tensor_tensor_scan(span(R, d, c1), span(CON[:, C_ONE:C_ONE + SEQ], d, 0),
                                              span(RQ[:, 0, :], d, c1), 0.0, ALU.mult, ALU.max)
            link(last)
            for d, at in ((0, P - 1), (1, P)):
                tt(one(MP, d, 0), one(B, d, at), one(R, d, at), ALU.add)
                last = ts(one(MP, d, 1), one(R, d, at), -1.0, None, ALU.mult)
            link(last)
            for d in range(2):
                c2 = 1 - d
                last = dve.tensor_tensor_scan(span(R, d, c2), span(CON[:, C_ONE:C_ONE + SEQ], d, 0),
                                              span(RQ[:, 0, :], d, c2), one(MP, d, 0), ALU.mult, ALU.max)
            link(last)
            link(tt(T2[0:ROW, :], B[0:ROW, :], R[0:ROW, :], ALU.add))
            dve.drain().then_inc(sem("scans_done"), 1)
            for u in range(U_V + 6, U_O):
                low(u)
            dve.wait_ge(sem("cols_turned"), 1)
            COLT, RSEL, Z, NS, DEN = (a_[n] for n in ("COLT", "RSEL", "Z", "NS", "DEN"))
            link(dve.tensor_copy(COLT, PS[:, 7, 0:8 * ROW].rearrange("p (a b) -> p a b", b=ROW)))

            def stage(h):
                for d in range(2):
                    last = ts(RSEL[0:ROW, h % 2, d * SEQ:(d + 1) * SEQ], R[0:ROW, :],
                              CON[0:ROW, C_ID + 32 * d + h:C_ID + 32 * d + h + 1], None, ALU.mult)
                last.then_inc(sem("r_staged"), 1)

            stage(0)
            low(U_O)
            for h in range(HEADS_A):
                def col(c, q, d):
                    return COLT[:, 4 * c + q, h + 32 * d:h + 32 * d + 1]

                u = U_O + 2 * h
                dve.wait_ge(sem("r_spread"), h + 1)
                for d in range(2):
                    for c in range(2):
                        last = stt(Z[:, d, c * P:(c + 1) * P], PS[:, 1, d * SEQ + c * P:d * SEQ + (c + 1) * P],
                                   col(c, 0, d), CON[:, C_MASK + d * P:C_MASK + (d + 1) * P], ALU.subtract, ALU.add)
                last.then_inc(sem("z_ready"), 1)
                low(u + 1)
                dve.wait_ge(sem("decay_ready"), h + 1)
                dve.wait_ge(sem("scores_a"), h + 1)
                if h:
                    dve.wait_ge(sem("intra_done"), 4 * h)
                tt(a_["DT"], Z, PS[:, 0:1, 0:SEQ].broadcast_to([P, 2, SEQ]), ALU.mult).then_inc(sem("dt_ready"), 1)
                if h + 1 < HEADS_A:
                    stage(h + 1)
                low(u + 2)
                dve.wait_ge(sem("inter_done"), h + 1)
                dve.wait_ge(sem("intra_ready"), 4 * h + 4)
                for d in range(2):
                    c = 1 - d
                    j = 2 * d + c
                    last = stt(NS[:, j, 0:DV_A + 1], PS[:, 3 + d, 0:DV_A + 1], col(c, 1, d),
                               NS[:, j, 0:DV_A + 1], ALU.mult, ALU.add)
                last.then_inc(sem("inter_read"), 1)
                dve.wait_ge(sem("inter_read"), h + 1)
                den = NS[:, :, DV_A:DV_A + 1]
                link(stt(DEN[:, 0:4].unsqueeze(2), den, -1.0, den, ALU.mult, ALU.max))
                for j in range(4):
                    d, c = divmod(j, 2)
                    last = ts(DEN[:, j:j + 1], DEN[:, j:j + 1], col(c, 2, d), None, ALU.max)
                link(last)
                link(dve.reciprocal(DEN[:, 4:8], DEN[:, 0:4]))
                for c in range(2):
                    last = ts(NS[:, c, 0:DV_A], NS[:, c, 0:DV_A], DEN[:, 4 + c:5 + c], None, ALU.mult)
                link(last)
                xh = [XN[:, c, h * DV_A:(h + 1) * DV_A] for c in range(2)]
                for c in range(2):
                    last = stt(xh[c], NS[:, 2 + c, 0:DV_A], DEN[:, 6 + c:7 + c], NS[:, c, 0:DV_A], ALU.mult, ALU.add)
                link(last)
                for c in range(2):
                    last = stt(NS[:, c, 0:DV_A], xh[c], 1.0, xh[c], ALU.mult, ALU.mult,
                               accum_out=SMA[:, 0, 8 * c + h:8 * c + h + 1])
                link(last)
                if h % 2:
                    dve.wait_ge(sem("o_free"), 2 + h + 1)
                    for t in range(NT):
                        xb = XN[:, t, (h - 1) * DV_A:(h + 1) * DV_A]
                        tt(xb, xb, a_["OGS"][:, t, :], ALU.mult).then_inc(sem("gated"), 1)
            ts(SMA[:, 0, :], SMA[:, 0, :], 1.0 / DV_A, EPS, ALU.mult, ALU.add).then_inc(sem("head_sums"), 1)
            dve.wait_ge(sem("gated"), HEADS_A)
            dve.wait_ge(sem("head_roots"), 1)
            link(dve.reciprocal(SMA[:, 1, :], SMA[:, 1, :]))
            for t in range(NT):
                xh = XN[:, t, :].rearrange("p (h v) -> p h v", h=HEADS_A)
                tt(xh, xh, SMA[:, 1, 8 * t:8 * t + 8].unsqueeze(2).broadcast_to([P, HEADS_A, DV_A]), ALU.mult)\
                    .then_inc(sem("xn_ready"), 1)
            low(U_AOUT + 1)
            turned("h", V_OUT, a_["T"])

            def residual(l, first, free, start, gain):
                dve.drain().then_inc(sem(free), 4)

                def add(b):
                    dve.wait_ge(sem("unit_used"), stream(first) + 4 * b + 4)
                    for t in range(NT):
                        xs = X[:, t, UNIT_C * b:UNIT_C * (b + 1)]
                        tt(xs, PS[:, OUT_BANKS[l][b][t], :], xs, ALU.add).then_inc(sem(free), 1)

                def columns(b):
                    for t in range(NT):
                        dve.wait_ge(sem("x_turned"), 8 * l + 2 * b + t + 1)
                        tt(m_["XT"][:, 4 * b:4 * b + 4, t * P:(t + 1) * P], ps4(4 + t), vec4(gain + 4 * b), ALU.mult)\
                            .then_inc(sem("x_columns"), 1)

                for n in range(start, 16):
                    low(first + n)
                    if n % 4 == 1 and n > 1:
                        add(n // 4 - 1)
                    if n % 4 == 3 and n > 3:
                        columns(n // 4 - 1)
                add(3)
                columns(3)
                dve.wait_ge(sem("square_parts"), 8 * (l + 1))
                link(red(SSQ[:, 0:2], SSB[:, :, :], AX.X, ALU.add))
                ts(SSQ[:, 2:4], SSQ[:, 0:2], 1.0 / D, EPS, ALU.mult, ALU.add).then_inc(sem("means"), 1)
                dve.wait_ge(sem("roots"), 2 * l + 2)
                dve.reciprocal(SSQ[:, 6:8], SSQ[:, 4:6]).then_inc(sem("ffn_norm"), 1)

            def route(l):
                SC, SR, MK, GATE, KEY = (m_[n] for n in ("SC", "SR", "MK", "GATE", "KEY"))
                G1, G2, G3, G4, G5, G6 = (m_[f"G{n}"] for n in range(1, 7))
                dve.wait_ge(sem("router_loaded"), 32)
                dve.wait_ge(sem("scores"), NT * (l + 1))
                link(tt(SR, SC, RB[:, :].unsqueeze(1).broadcast_to([P, NT, N_EXP]), ALU.add))
                lt = CON[:, C_LT:C_LT + 16].rearrange("p (j i) -> p j i", j=4)
                grp = NT * N_GRP
                full = [P, grp, 4, 4]
                g1, g2 = (g.rearrange("p (g j i) -> p g j i", g=grp, j=4) for g in (G1, G2))
                sg = SR.rearrange("p t (g e) -> p (t g) e", g=N_GRP)
                si, sj = sg.unsqueeze(2).broadcast_to(full), sg.unsqueeze(3).broadcast_to(full)
                tt(g1, si, sj, ALU.is_gt)
                link(tt(g2, si, sj, ALU.is_equal))
                link(tt(g2, g2, lt.unsqueeze(1).broadcast_to(full), ALU.mult))
                link(tt(G1, G1, G2, ALU.add))
                link(red(G3, G1.rearrange("p (a i) -> p a i", i=4), AX.X, ALU.add))
                link(ts(G4, G3, 1.5, None, ALU.is_lt))
                link(tt(G5, G4, SR.rearrange("p t e -> p (t e)"), ALU.mult))
                link(red(G6[:, 0:8], G5.rearrange("p (a i) -> p a i", i=4), AX.X, ALU.add))
                gs = G6[:, 0:8].rearrange("p (t g) -> p t g", t=NT)
                four = [P, NT, 4, 4]
                h1, h2 = (g[:, 0:32].rearrange("p (t j i) -> p t j i", t=NT, j=4) for g in (G1, G2))
                gi, gj = gs.unsqueeze(2).broadcast_to(four), gs.unsqueeze(3).broadcast_to(four)
                tt(h1, gi, gj, ALU.is_gt)
                link(tt(h2, gi, gj, ALU.is_equal))
                link(tt(h2, h2, lt.unsqueeze(1).broadcast_to(four), ALU.mult))
                link(tt(h1, h1, h2, ALU.add))
                link(red(G6[:, 8:16], G1[:, 0:32].rearrange("p (a i) -> p a i", i=4), AX.X, ALU.add))
                link(ts(G6[:, 16:24], G6[:, 8:16], 0.5, None, ALU.is_lt))
                link(tt(MK.rearrange("p t (g e) -> p (t g) e", g=4), G4.rearrange("p (g e) -> p g e", g=grp),
                        G6[:, 16:24].unsqueeze(2).broadcast_to([P, grp, 4]), ALU.mult))
                dve.drain().then_inc(sem("mask_ready"), 1)
                link(tt(GATE, MK, SC, ALU.mult))
                link(red(G5[:, 0:2], GATE, AX.X, ALU.add))
                link(dve.reciprocal(G5[:, 2:4], G5[:, 0:2]))
                link(tt(GATE, GATE, G5[:, 2:4].unsqueeze(2).broadcast_to([P, NT, N_EXP]), ALU.mult))
                dve.wait_ge(sem("positions"), l + 1)
                pos = PS[:, 1, 0:NT * N_EXP].rearrange("p (t e) -> p t e", t=NT)
                red(G5[:, 4:5], PS[:, 1, NT * N_EXP:3 * N_EXP], AX.X, ALU.max)
                link(stt(KEY, pos, 1.0, MK, ALU.add, ALU.mult))
                link(ts(KEY, KEY, -1.0, None, ALU.add))
                ts(FLAG[:, l:l + 1], G5[:, 4:5], float(SLOTS), None, ALU.is_gt).then_inc(sem("routed"), 1)
                dve.wait_ge(sem("routed"), l + 1)

            def experts(l, gain, done):
                SEL, SELG, KEY, GATE = m_["SEL"], m_["SELG"], m_["KEY"], m_["GATE"]

                def select(m, j, i, first):
                    for t in range(NT):
                        for e in range(2):
                            last = ts(SEL[:, t, SLOTS * e:SLOTS * (e + 1)], CON[:, ds(C_IOTA + first, SLOTS)],
                                      KEY[:, t, ds(2 * i + e, 1)], None, ALU.is_equal)
                    last.then_inc(sem(m + "sel_ready"), 1)

                def select_gated(m, j, i, first):
                    for t in range(NT):
                        for e in range(2):
                            ts(SELG[:, t, SLOTS * e:SLOTS * (e + 1)], CON[:, ds(C_IOTA + first, SLOTS)],
                                      KEY[:, t, ds(2 * i + e, 1)], GATE[:, t, ds(2 * i + e, 1)], ALU.is_equal, ALU.mult)

                def gathered(m, j):
                    for g in range(4):
                        dve.wait_ge(sem(m + "gathered"), 4 * j + g + 1)
                        tt(m_["XG"][:, 4 * g:4 * g + 4, :], ps4(2 + g % 2), vec4(gain + 4 * g), ALU.mult)\
                            .then_inc(sem(m + "xg_ready"), 1)

                def pair(m, j, following, i, first):
                    if following:
                        select(m, j + 1, i + 1, first)
                    select_gated(m, j, i, first)
                    dve.wait_ge(sem(m + "sig"), j + 1)
                    tt(m_["SIG"], PS[:, 0, :], m_["SIG"], ALU.mult).then_inc(sem(m + "silu"), 1)
                    dve.wait_ge(sem(m + "silu"), j + 1)
                    tt(m_["A"], PS[:, 1, :], m_["SIG"], ALU.mult).then_inc(sem(m + "a_ready"), 1)
                    if following:
                        gathered(m, j + 1)
                    dve.wait_ge(sem(m + "sel_turned"), j + 1)
                    dve.tensor_copy(m_["SCT"], PS[:, 5, 0:SEQ]).then_inc(sem(m + "sct_ready"), 1)
                    for d in range(4):
                        for t in range(NT):
                            dve.wait_ge(sem(m + "scattered"), 8 * j + 2 * d + t + 1)
                            xs = X[:, t, d * UNIT_C:(d + 1) * UNIT_C]
                            tt(xs, PS[:, 2 + t, :], xs, ALU.add).then_inc(sem(m + "x_added"), 1)

                m = "m_"
                first = PAIRS * l
                select(m, first, 0, 0)
                gathered(m, first)
                with dve.Fori(0, PAIRS - 1) as i:
                    pair(m, i + first, True, i, 0)
                pair(m, PAIRS - 1 + first, False, PAIRS - 1, 0)
                m = f"o{l}_"
                flag = dve.value_load(FLAG[0:1, l:l + 1], min_val=0, max_val=1)
                with dve.If(flag > 0):
                    dve.drain().then_inc(sem(f"over_free_{l}"), 4)
                    with dve.Fori(0, EXTRA) as q:
                        with dve.Fori(0, PAIRS) as i:
                            j = q * PAIRS + i
                            first = (q + 1) * SLOTS
                            select(m, j, i, first)
                            gathered(m, j)
                            pair(m, j, False, i, first)
                dve.drain().then_inc(sem(done), 1)

            residual(0, U_AOUT, "aout_free", 2, V_FFN)
            route(0)
            experts(0, V_FFN, "x_ready")

            low(S_CKV)
            low(S_CKV + 1)
            norm("n2")
            turned("n2", V_MIX + 16, b_["T"])
            dve.wait_ge(sem("few_hi"), 2)
            tt(WKRP[1][:, :, :], b_["WKR"], WKRP[0][:, :, :], ALU.subtract).then_inc(sem("few_lo"), 1)
            low(S_CKV + 2)
            low(S_CKV + 3)
            low(S_PAIRS)
            CKV, KR, KRT, KRR, QG, KG, SS, RN = (b_[n] for n in ("CKV", "KR", "KRT", "KRR", "QG", "KG", "SS", "RN"))
            QP, KVP = b_["QP"], b_["KVP"]
            COS = CON[:, C_COS:C_COS + 2 * ROPE].rearrange("p (t r) -> p t r", t=NT)
            SIN = CON[:, C_SIN:C_SIN + 2 * ROPE].rearrange("p (t r) -> p t r", t=NT)

            def swapped(v):
                return v.rearrange("p t (a r) -> p t a r", a=2)[:, :, ::-1, :]

            def halves(v):
                return v.rearrange("p t (a r) -> p t a r", a=2)

            dve.wait_ge(sem("ckv_copied"), 2)
            for t in range(NT):
                link(tt(b_["JUNK"][:, 0:RANK], CKV[:, t, :], CKV[:, t, :], ALU.mult))
                link(red(SSQ[:, t:t + 1], b_["JUNK"][:, 0:RANK], AX.X, ALU.add))
            ts(SSQ[:, 2:4], SSQ[:, 0:2], 1.0 / RANK, EPS, ALU.mult, ALU.add).then_inc(sem("ckv_means"), 1)
            low(S_PAIRS + 1)
            dve.wait_ge(sem("ckv_roots"), 1)
            link(dve.reciprocal(SSQ[:, 6:8], SSQ[:, 4:6]))
            for t in range(NT):
                ts(CKV[:, t, :], CKV[:, t, :], SSQ[:, 6 + t:7 + t], None, ALU.mult).then_inc(sem("ckv_normed"), 1)
            low(S_PAIRS + 2)
            dve.wait_ge(sem("ckv_turned"), 1)
            for t in range(NT):
                tt(b_["T"][:, t, :].rearrange("p (a b) -> p a b", a=4), ps4(2 + t), vec4(V_KV), ALU.mult)\
                    .then_inc(sem("ckt_tmp"), 1)
            for t in range(NT):
                dve.wait_ge(sem("ckt_hi"), t + 1)
                tt(CKL[:, :, t * P:(t + 1) * P], b_["T"][:, t, :].rearrange("p (a b) -> p a b", a=4),
                   CKH[:, :, t * P:(t + 1) * P], ALU.subtract).then_inc(sem("ckt_ready"), 1)
            low(S_PAIRS + 3)
            low(S_PAIRS + 4)
            dve.wait_ge(sem("qk_gains"), 32)
            link(tt(KRR, KR, KR, ALU.mult))
            link(red(MPB[:, 0:2], KRR, AX.X, ALU.add))
            link(tt(KR, KR, KG[:, NOPE:DQ_B].unsqueeze(1).broadcast_to([P, NT, ROPE]), ALU.mult))
            link(tt(halves(KRT), swapped(KR), halves(SIN), ALU.mult))
            link(tt(KR, KR, COS, ALU.mult))
            link(tt(KRR, KR, KRT, ALU.add))
            low(S_PAIRS + 5)

            def sums(i):
                sq = SQ[:, 0:NT * PAIR_Q].rearrange("p (t c) -> p t c", t=NT)
                dve.wait_ge(sem("q_read"), 2 * i + 2)
                link(tt(sq, QP, QP, ALU.mult))
                link(red(SS[:, 0:4], SQ[:, 0:NT * PAIR_Q].rearrange("p (a c) -> p a c", a=4), AX.X, ALU.add))
                dve.wait_ge(sem("kv_read"), 2 * i + 2)
                for t in range(NT):
                    k = KVP[:, 2 * (i % 2) + t, :].rearrange("p (h c) -> p h c", h=2)[:, :, 0:NOPE]
                    last = tt(SQ[:, 2 * NOPE * t:2 * NOPE * (t + 1)].rearrange("p (h c) -> p h c", h=2), k, k, ALU.mult)
                link(last)
                link(red(SS[:, 4:8], SQ[:, 0:4 * NOPE].rearrange("p (a c) -> p a c", a=4), AX.X, ALU.add))
                ss = SS[:, 4:8].rearrange("p (t h) -> p t h", t=NT)
                link(tt(ss, ss, MPB[:, :].unsqueeze(2).broadcast_to([P, NT, 2]), ALU.add))
                ts(SS, SS, 1.0 / DQ_B, EPS, ALU.mult, ALU.add).then_inc(sem("qk_means"), 1)

            def normed(i):
                dve.wait_ge(sem("qk_roots"), i + 1)
                link(dve.reciprocal(RN, b_["RT"]))
                link(ts(RN[:, 0:4], RN[:, 0:4], DQ_B ** -0.5, None, ALU.mult))
                for p in range(2):
                    for t in range(NT):
                        stt(QN[p][:, t, :], QP[:, t, p * DQ_B:(p + 1) * DQ_B], RN[:, 2 * t + p:2 * t + p + 1], QG,
                            ALU.mult, ALU.mult)
                        stt(KN[p][:, t, 0:NOPE], KVP[:, 2 * (i % 2) + t, 2 * P * p:2 * P * p + NOPE],
                            RN[:, 4 + 2 * t + p:5 + 2 * t + p], KG[:, 0:NOPE], ALU.mult, ALU.mult)
                        last = ts(KN[p][:, t, NOPE:DQ_B], KRR[:, t, :], RN[:, 4 + 2 * t + p:5 + 2 * t + p], None, ALU.mult)
                    link(last)
                    qr = QN[p][:, :, NOPE:DQ_B]
                    tt(halves(ROT[p]), swapped(qr), halves(SIN), ALU.mult)
                    link(tt(ROS[p], qr, COS, ALU.mult))
                    tt(qr, ROT[p], ROS[p], ALU.add).then_inc(sem("qk_normed"), 1)

            for i in range(HEADS_B // 2):
                more = i + 1 < HEADS_B // 2
                s = S_PAIRS + 5 * (i + 1)
                low(s + 1)
                sums(i)
                if more:
                    low(s + 2)
                normed(i)
                if more:
                    low(s + 3)
                for p in range(2):
                    h = 2 * i + p
                    dve.wait_ge(sem("scores_b"), h + 1)
                    red(SM[:, p, 0:2], PS[:, 4 + p, :].rearrange("p (t s) -> p t s", t=NT), AX.X, ALU.max,
                        negate=True).then_inc(sem("max_ready"), 1)
                for p in range(2):
                    h = 2 * i + p
                    dve.wait_ge(sem("exp_done"), 2 * h + 2)
                    link(dve.reciprocal(SM[:, p, 4:6], SM[:, p, 2:4]))
                    tt(PR[p], PR[p], SM[:, p, 4:6].unsqueeze(2).broadcast_to([P, NT, SEQ]), ALU.mult)\
                        .then_inc(sem("probs_ready"), 1)
                if more:
                    low(s + 4)
                    low(s + 5)
                else:
                    low(s + 2)
                    low(s + 3)
            dve.wait_ge(sem("o_copied"), HEADS_B)

            residual(1, S_BOUT, "bout_free", 4, V_FFN + 16)
            route(1)
            experts(1, V_FFN + 16, "x_ready")


_WEIGHTS = ["x", "norm_mix", "norm_ffn", "a_w_in", "a_conv_w", "a_gate_b", "a_out_norm", "a_w_out",
            "b_w_in", "b_kv_norm", "b_w_ukv", "b_q_norm", "b_k_norm", "b_w_out", "router_w", "router_b",
            "moe_w_gate", "moe_w_up", "moe_w_down"]


def constants():
    import numpy as np
    c = np.zeros((P, C_ALL), np.float32)
    p, f = np.arange(P)[:, None], np.arange(P)[None, :]
    c[:, C_ID:C_ID + P] = p == f
    c[:, C_TRI:C_TRI + P] = p < f
    c[:, C_ONE:C_ONE + P] = 1.0
    c[:, C_IOTA:C_IOTA + SEQ] = np.arange(SEQ)
    c[:, C_MASK:C_MASK + P] = np.where(p <= f, 0.0, MASKED)
    c[:, C_MASK + P:C_MASK + 2 * P] = np.where(p >= f, 0.0, MASKED)
    c[:, C_LT:C_LT + 16] = np.array([[i < j for i in range(4)] for j in range(4)]).reshape(-1)
    inv = np.float32(10000.0) ** (-np.arange(HALF, dtype=np.float32) / HALF)
    for t in range(NT):
        ang = (np.arange(P, dtype=np.float32) + t * P)[:, None] * inv[None, :].astype(np.float32)
        cos, sin = np.cos(ang), np.sin(ang)
        c[:, C_COS + t * ROPE:C_COS + (t + 1) * ROPE] = np.concatenate([cos, cos], 1)
        c[:, C_SIN + t * ROPE:C_SIN + (t + 1) * ROPE] = np.concatenate([-sin, sin], 1)
    return c


def kernel(**inputs):
    import numpy as np
    import concourse.bacc as bacc
    from concourse.bass_utils import run_bass_kernel_spmd

    nc = bacc.Bacc("TRN2", target_bir_lowering=False, num_devices=1)
    arrays = {f"in_{n}": np.ascontiguousarray(inputs[n]) for n in _WEIGHTS}
    arrays["in_consts"] = constants()
    w = {n[3:]: nc.dram_tensor(n, a.shape, mybir.dt.float32, kind="ExternalInput").ap() for n, a in arrays.items()}
    out = nc.dram_tensor("out", (1, SEQ, D), mybir.dt.float32, kind="ExternalOutput").ap()
    trunk(nc, w, out)
    r = run_bass_kernel_spmd(nc, [arrays], core_ids=[0])
    return r.results[0]["out"]
```
